# Optimizing a Trainium2 kernel written in Bass

```python
import jax
import jax.numpy as jnp
from jax import lax
import numpy as np
import jax, jax.numpy as jnp

D_MODEL = 1024
BATCH = 1
SEQ = 512
DEPTH = 1

CHUNK = 64
HEAD_DIM = 64
D_RWKV = 512
D_ATT = 512
D_MIX = D_RWKV + D_ATT
N_RWKV_HEADS = D_RWKV // HEAD_DIM
N_ATT_HEADS = D_ATT // HEAD_DIM
LORA_W = 64
LORA_A = 64
N_LEFT_CHUNKS = 8
BAND = (N_LEFT_CHUNKS + 1) * CHUNK
REL_CLIP = 128
N_REL = CHUNK + REL_CLIP
RMS_EPS = 1e-6
GN_EPS = 64e-5
D_SHIFT = 4 * D_RWKV + LORA_W + LORA_A
D_IN = D_SHIFT + 4 * D_ATT


def rms_norm(x, g):
    x32 = x.astype(jnp.float32)
    y = x32 * lax.rsqrt(jnp.mean(x32 * x32, axis=-1, keepdims=True) + RMS_EPS)
    return y.astype(x.dtype) * g

def token_shift(p, mu):
    prev = jnp.pad(p, ((0, 0), (1, 0), (0, 0)))[:, :-1]
    return p + mu * (prev - p)

def rwkv7_step(state, inp):
    r_t, w_t, k_t, v_t, a_t, b_t = inp
    sa = jnp.einsum('bhij,bhj->bhi', state, a_t)
    state = state * w_t[:, :, None, :] + sa[..., None] * b_t[:, :, None, :] + v_t[..., None] * k_t[:, :, None, :]
    y = jnp.einsum('bhij,bhj->bhi', state, r_t)
    return state, y

def rwkv7_mix(ps, w0, w2, a0, a2, k_k, k_a, r_k, lnx_g, lnx_b):
    b_, s_, _ = ps.shape
    f32 = jnp.float32
    r, k, v, g, wd, ad = jnp.split(ps, [D_RWKV, 2 * D_RWKV, 3 * D_RWKV, 4 * D_RWKV, 4 * D_RWKV + LORA_W], axis=-1)
    w_log = -jax.nn.softplus(-(w0 + jnp.tanh(wd) @ w2).astype(f32)) - 0.5
    decay = jnp.exp(-jnp.exp(w_log))
    a = jax.nn.sigmoid((a0 + ad @ a2).astype(f32))
    heads = lambda t: t.astype(f32).reshape(b_, s_, N_RWKV_HEADS, HEAD_DIM)
    r, k, v, decay, a = heads(r), heads(k), heads(v), heads(decay), heads(a)
    kk = k * k_k.astype(f32).reshape(N_RWKV_HEADS, HEAD_DIM)
    kk = kk / jnp.maximum(jnp.sqrt(jnp.sum(kk * kk, axis=-1, keepdims=True)), 1e-12)
    k = k * (1.0 + (a - 1.0) * k_a.astype(f32).reshape(N_RWKV_HEADS, HEAD_DIM))
    seq_first = lambda t: jnp.moveaxis(t, 1, 0)
    state0 = jnp.zeros((b_, N_RWKV_HEADS, HEAD_DIM, HEAD_DIM), f32)
    _, y = lax.scan(rwkv7_step, state0, (seq_first(r), seq_first(decay), seq_first(k), seq_first(v), seq_first(-kk), seq_first(kk * a)))
    y = jnp.moveaxis(y, 0, 1)
    mean = jnp.mean(y, axis=-1, keepdims=True)
    yc = y - mean
    y = yc * lax.rsqrt(jnp.mean(yc * yc, axis=-1, keepdims=True) + GN_EPS)
    y = y.reshape(b_, s_, D_RWKV) * lnx_g.astype(f32) + lnx_b.astype(f32)
    bonus = jnp.sum(r * k * r_k.astype(f32), axis=-1, keepdims=True) * v
    y = y + bonus.reshape(b_, s_, D_RWKV)
    return y.astype(ps.dtype), g

def chunk_band_attention(q, k, v, q_g, k_g, rel_bias):
    b_, s_, _ = q.shape
    nc = s_ // CHUNK
    pad = N_LEFT_CHUNKS * CHUNK
    def heads(t):
        return t.reshape(b_, s_, N_ATT_HEADS, HEAD_DIM).transpose(0, 2, 1, 3)
    q = heads(rms_norm(q.reshape(b_, s_, N_ATT_HEADS, HEAD_DIM), q_g).reshape(b_, s_, D_ATT))
    k = heads(rms_norm(k.reshape(b_, s_, N_ATT_HEADS, HEAD_DIM), k_g).reshape(b_, s_, D_ATT))
    v = heads(v)
    qc = q.reshape(b_, N_ATT_HEADS, nc, CHUNK, HEAD_DIM)
    def band(t):
        tp = jnp.pad(t, ((0, 0), (0, 0), (pad, 0), (0, 0))).reshape(b_, N_ATT_HEADS, nc + N_LEFT_CHUNKS, CHUNK, HEAD_DIM)
        return jnp.concatenate([tp[:, :, i:i + nc] for i in range(N_LEFT_CHUNKS + 1)], axis=3)
    kb, vb = band(k), band(v)
    s = jnp.einsum('bhnqd,bhnkd->bhnqk', qc, kb).astype(jnp.float32) * (HEAD_DIM ** -0.5)
    dist = jnp.arange(CHUNK)[:, None] + pad - jnp.arange(BAND)[None, :]
    rel_idx = jnp.clip(dist, -(CHUNK - 1), REL_CLIP) + (CHUNK - 1)
    bias = rel_bias[:, rel_idx].astype(jnp.float32)
    valid = (jnp.arange(nc)[:, None] * CHUNK + jnp.arange(BAND)[None, :] - pad) >= 0
    s = s + bias[None, :, None]
    s = jnp.where(valid[None, None, :, None, :], s, -1e30)
    p = jax.nn.softmax(s, axis=-1).astype(v.dtype)
    o = jnp.einsum('bhnqk,bhnkd->bhnqd', p, vb)
    return o.reshape(b_, N_ATT_HEADS, s_, HEAD_DIM).transpose(0, 2, 1, 3).reshape(b_, s_, D_ATT)

def first_inputs(seed: int = 0) -> dict:
    key = jax.random.key(seed)
    ks = jax.random.split(key, 22)
    n = lambda i, shape: jax.random.normal(ks[i], shape, jnp.float32)
    L = DEPTH
    return {
        'x': n(0, (BATCH, SEQ, D_MODEL)),
        'c': n(1, (BATCH, D_MODEL)),
        'norm_g': 1.0 + 0.1 * n(2, (L, D_MODEL)),
        'w_ada': n(3, (L, D_MODEL, 3 * D_MODEL)) * (0.5 * D_MODEL ** -0.5),
        'b_ada': 0.02 * n(4, (L, 3 * D_MODEL)),
        'w_in': n(5, (L, D_MODEL, D_IN)) * (D_MODEL ** -0.5),
        'mu_shift': jax.random.uniform(ks[6], (L, D_SHIFT), jnp.float32),
        'w0': -1.0 + 0.5 * n(7, (L, D_RWKV)),
        'w2': n(8, (L, LORA_W, D_RWKV)) * (0.5 * LORA_W ** -0.5),
        'a0': 0.5 * n(9, (L, D_RWKV)),
        'a2': n(10, (L, LORA_A, D_RWKV)) * (0.5 * LORA_A ** -0.5),
        'k_k': 0.85 + 0.05 * n(11, (L, D_RWKV)),
        'k_a': 1.0 + 0.05 * n(12, (L, D_RWKV)),
        'r_k': 0.1 * n(13, (L, N_RWKV_HEADS, HEAD_DIM)),
        'lnx_g': 1.0 + 0.1 * n(14, (L, D_RWKV)),
        'lnx_b': 0.02 * n(15, (L, D_RWKV)),
        'q_norm_g': 1.0 + 0.1 * n(16, (L, HEAD_DIM)),
        'k_norm_g': 1.0 + 0.1 * n(17, (L, HEAD_DIM)),
        'rel_bias': 0.5 * n(18, (L, N_ATT_HEADS, N_REL)),
        'w_out': n(19, (L, D_MIX, D_MODEL)) * (D_MIX ** -0.5),
    }

def first_block(x, c, norm_g, w_ada, b_ada, w_in, mu_shift, w0, w2, a0, a2, k_k, k_a, r_k, lnx_g, lnx_b, q_norm_g, k_norm_g, rel_bias, w_out):
    c_act = jax.nn.silu(c)
    for l in range(DEPTH):
        mod = c_act @ w_ada[l] + b_ada[l]
        shift, scale, gate = jnp.split(mod, 3, axis=-1)
        h = rms_norm(x, norm_g[l]) * (1.0 + scale[:, None, :]) + shift[:, None, :]
        proj = h @ w_in[l]
        ps = token_shift(proj[..., :D_SHIFT], mu_shift[l])
        pa = proj[..., D_SHIFT:]
        y_r, g_r = rwkv7_mix(ps, w0[l], w2[l], a0[l], a2[l], k_k[l], k_a[l], r_k[l], lnx_g[l], lnx_b[l])
        q, ka, va, g_a = jnp.split(pa, 4, axis=-1)
        y_a = chunk_band_attention(q, ka, va, q_norm_g[l], k_norm_g[l], rel_bias[l])
        y = jnp.concatenate([y_r * jax.nn.silu(g_r), y_a * jax.nn.silu(g_a)], axis=-1)
        x = x + gate[:, None, :] * (y @ w_out[l])
    return x


D_MIX_2 = D_MODEL
SSD_WIDTH = D_MIX_2 // 2
SSD_HEAD_DIM = 64
SSD_HEADS = SSD_WIDTH // SSD_HEAD_DIM
SSD_GROUPS = 2
SSD_STATE = 128
SSD_CONV = 4
SSD_CHUNK = 128
ATTN_WIDTH = D_MIX_2 // 4
ATTN_HEAD_DIM = 64
ATTN_HEADS = ATTN_WIDTH // ATTN_HEAD_DIM
ATTN_BLOCK = 128
CONV_WIDTH = D_MIX_2 - SSD_WIDTH - ATTN_WIDTH
CONV_KERNEL = 31
XBC_WIDTH = SSD_WIDTH + 2 * SSD_GROUPS * SSD_STATE
D_IN_2 = SSD_WIDTH + XBC_WIDTH + SSD_HEADS + 3 * ATTN_WIDTH + ATTN_HEADS + 2 * CONV_WIDTH
N_EXPERT_GROUPS = 4
EXPERTS_PER_GROUP = 8
N_EXPERTS = N_EXPERT_GROUPS * EXPERTS_PER_GROUP
TOP_K = 2
D_EXPERT = 512
MOE_BLOCK = 256
NORM_EPS = 1e-6


def _rms(x):
    xf = x.astype(jnp.float32)
    return xf * lax.rsqrt(jnp.mean(xf * xf, axis=-1, keepdims=True) + NORM_EPS)

def rms_norm_2(x, g):
    return (_rms(x) * g.astype(jnp.float32)).astype(x.dtype)

def layer_norm(x, g, b):
    xf = x.astype(jnp.float32)
    mu = jnp.mean(xf, axis=-1, keepdims=True)
    var = jnp.mean(jnp.square(xf - mu), axis=-1, keepdims=True)
    y = (xf - mu) * lax.rsqrt(var + NORM_EPS) * g.astype(jnp.float32) + b.astype(jnp.float32)
    return y.astype(x.dtype)

def causal_depthwise_conv(x, w, b):
    k = w.shape[0]
    y = lax.conv_general_dilated(
        x, w[:, None, :].astype(x.dtype), window_strides=(1,), padding=[(k - 1, 0)],
        dimension_numbers=('NWC', 'WIO', 'NWC'), feature_group_count=x.shape[-1])
    return y + b.astype(x.dtype)

def ssd_mixer(z, xbc, dt_raw, conv_w, conv_b, dt_bias, a_log, d_skip, norm_g):
    f32 = jnp.float32
    bsz, seq, _ = z.shape
    nc = seq // SSD_CHUNK
    r = SSD_HEADS // SSD_GROUPS
    gn = SSD_GROUPS * SSD_STATE
    xbc = jax.nn.silu(causal_depthwise_conv(xbc, conv_w, conv_b))
    xs, bmat, cmat = jnp.split(xbc, [SSD_WIDTH, SSD_WIDTH + gn], axis=-1)
    dt = jax.nn.softplus(dt_raw.astype(f32) + dt_bias.astype(f32))
    a = -jnp.exp(a_log.astype(f32))
    x_h = xs.reshape(bsz, nc, SSD_CHUNK, SSD_GROUPS, r, SSD_HEAD_DIM).astype(f32)
    dt_c = dt.reshape(bsz, nc, SSD_CHUNK, SSD_GROUPS, r)
    xdt = x_h * dt_c[..., None]
    bm = bmat.reshape(bsz, nc, SSD_CHUNK, SSD_GROUPS, SSD_STATE).astype(f32)
    cm = cmat.reshape(bsz, nc, SSD_CHUNK, SSD_GROUPS, SSD_STATE).astype(f32)
    acs = jnp.cumsum(dt_c * a.reshape(SSD_GROUPS, r), axis=2)
    acs = acs.transpose(0, 1, 3, 4, 2)
    causal = jnp.tril(jnp.ones((SSD_CHUNK, SSD_CHUNK), dtype=bool))
    decay_in = jnp.exp(jnp.where(causal, acs[..., :, None] - acs[..., None, :], -jnp.inf))
    cb = jnp.einsum('bclgn,bcsgn->bcgls', cm, bm)
    y_diag = jnp.einsum('bcgls,bcgrls,bcsgrp->bclgrp', cb, decay_in, xdt)
    decay_to_end = jnp.exp(acs[..., -1:] - acs)
    states = jnp.einsum('bclgn,bcgrl,bclgrp->bcgrpn', bm, decay_to_end, xdt)
    chunk_decay = jnp.exp(acs[..., -1])

    def step(h, inp):
        st, dec = inp
        return h * dec[..., None, None] + st, h

    h0 = jnp.zeros_like(states[:, 0])
    _, prev = lax.scan(step, h0, (states.swapaxes(0, 1), chunk_decay.swapaxes(0, 1)))
    prev = prev.swapaxes(0, 1)
    y_off = jnp.einsum('bclgn,bcgrpn,bcgrl->bclgrp', cm, prev, jnp.exp(acs))
    y = y_diag + y_off + x_h * d_skip.astype(f32).reshape(SSD_GROUPS, r, 1)
    y = y.reshape(bsz, seq, SSD_GROUPS, r * SSD_HEAD_DIM)
    y = y * jax.nn.silu(z.astype(f32)).reshape(bsz, seq, SSD_GROUPS, r * SSD_HEAD_DIM)
    y = _rms(y).reshape(bsz, seq, SSD_WIDTH) * norm_g.astype(f32)
    return y.astype(z.dtype)

def forgetting_attention(q, k, v, f_logit, f_bias, norm_g):
    f32 = jnp.float32
    bsz, seq, _ = q.shape
    nb = seq // ATTN_BLOCK
    scale = ATTN_HEAD_DIM ** -0.5
    qh = q.reshape(bsz, seq, ATTN_HEADS, ATTN_HEAD_DIM).transpose(0, 2, 1, 3)
    kh = k.reshape(bsz, seq, ATTN_HEADS, ATTN_HEAD_DIM).transpose(0, 2, 1, 3)
    vh = v.reshape(bsz, seq, ATTN_HEADS, ATTN_HEAD_DIM).transpose(0, 2, 1, 3)
    log_f = jax.nn.log_sigmoid(f_logit.astype(f32) + f_bias.astype(f32))
    cum = jnp.cumsum(log_f, axis=1).transpose(0, 2, 1)
    qb = qh.reshape(bsz, ATTN_HEADS, nb, ATTN_BLOCK, ATTN_HEAD_DIM).transpose(2, 0, 1, 3, 4)
    cb = cum.reshape(bsz, ATTN_HEADS, nb, ATTN_BLOCK).transpose(2, 0, 1, 3)
    k_pos = jnp.arange(seq)

    def block(args):
        qi, ci, i = args
        s = jnp.einsum('bhqd,bhkd->bhqk', qi, kh).astype(f32) * scale
        s = s + ci[..., :, None] - cum[:, :, None, :]
        q_pos = i * ATTN_BLOCK + jnp.arange(ATTN_BLOCK)
        s = jnp.where(k_pos[None, :] <= q_pos[:, None], s, -jnp.inf)
        p = jax.nn.softmax(s, axis=-1)
        return jnp.einsum('bhqk,bhkd->bhqd', p.astype(vh.dtype), vh)

    o = lax.map(block, (qb, cb, jnp.arange(nb)))
    o = o.transpose(1, 0, 3, 2, 4).reshape(bsz, seq, ATTN_WIDTH)
    return rms_norm_2(o, norm_g)

def conformer_conv(glu_a, glu_b, conv_w, conv_b, ln_g, ln_b):
    u = glu_a * jax.nn.sigmoid(glu_b)
    u = causal_depthwise_conv(u, conv_w, conv_b)
    u = layer_norm(u, ln_g, ln_b)
    return jax.nn.silu(u)

def hybrid_mixer(h, w_in, ssd_conv_w, ssd_conv_b, ssd_dt_bias, ssd_a_log, ssd_d, ssd_norm_g,
                 fox_f_bias, fox_norm_g, cm_conv_w, cm_conv_b, cm_ln_g, cm_ln_b, w_out):
    sizes = (SSD_WIDTH, XBC_WIDTH, SSD_HEADS, ATTN_WIDTH, ATTN_WIDTH, ATTN_WIDTH,
             ATTN_HEADS, CONV_WIDTH, CONV_WIDTH)
    splits = np.cumsum(sizes)[:-1].tolist()
    proj = h @ w_in
    z, xbc, dt_raw, q, k, v, f_logit, glu_a, glu_b = jnp.split(proj, splits, axis=-1)
    y_ssd = ssd_mixer(z, xbc, dt_raw, ssd_conv_w, ssd_conv_b, ssd_dt_bias, ssd_a_log, ssd_d, ssd_norm_g)
    y_att = forgetting_attention(q, k, v, f_logit, fox_f_bias, fox_norm_g)
    y_cnv = conformer_conv(glu_a, glu_b, cm_conv_w, cm_conv_b, cm_ln_g, cm_ln_b)
    y = jnp.concatenate([y_ssd.astype(h.dtype), y_att.astype(h.dtype), y_cnv.astype(h.dtype)], axis=-1)
    return y @ w_out

def hierarchical_moe(h, w_rg, b_rg, w_re, b_re, w_gate, w_up, w_down):
    f32 = jnp.float32
    bsz, seq, d = h.shape
    m = bsz * seq
    hf = h.reshape(m, d)
    p_g = jax.nn.softmax((hf @ w_rg + b_rg).astype(f32), axis=-1)
    g_sel = jnp.argmax(p_g, axis=-1).astype(jnp.int32)
    p_gsel = jnp.take_along_axis(p_g, g_sel[:, None], axis=-1)
    e_logits = (hf @ w_re + b_re).astype(f32).reshape(m, N_EXPERT_GROUPS, EXPERTS_PER_GROUP)
    e_logits = jnp.take_along_axis(e_logits, g_sel[:, None, None], axis=1)[:, 0]
    top_p, top_i = lax.top_k(jax.nn.softmax(e_logits, axis=-1), TOP_K)
    weights = top_p / jnp.sum(top_p, axis=-1, keepdims=True) * p_gsel
    expert = g_sel[:, None] * EXPERTS_PER_GROUP + top_i.astype(jnp.int32)
    n_assign = m * TOP_K
    flat_e = expert.reshape(-1)
    flat_w = weights.reshape(-1)
    flat_tok = jnp.arange(n_assign, dtype=jnp.int32) // TOP_K
    order = jnp.argsort(flat_e)
    se, stok, sw = flat_e[order], flat_tok[order], flat_w[order]
    counts = jnp.zeros((N_EXPERTS,), jnp.int32).at[flat_e].add(1)
    padded = (counts + MOE_BLOCK - 1) // MOE_BLOCK * MOE_BLOCK
    start = jnp.cumsum(counts) - counts
    pad_end = jnp.cumsum(padded)
    pad_start = pad_end - padded
    dest = pad_start[se] + jnp.arange(n_assign, dtype=jnp.int32) - start[se]
    n_blocks = (n_assign + MOE_BLOCK - 1) // MOE_BLOCK + N_EXPERTS
    rows = n_blocks * MOE_BLOCK
    xs = jnp.zeros((rows, d), h.dtype).at[dest].set(hf[stok])
    block_e = jnp.minimum(
        jnp.searchsorted(pad_end, jnp.arange(n_blocks, dtype=jnp.int32) * MOE_BLOCK, side='right'),
        N_EXPERTS - 1)

    def expert_block(args):
        xb, e = args
        hid = jax.nn.silu(xb @ w_gate[e]) * (xb @ w_up[e])
        return hid @ w_down[e]

    ys = lax.map(expert_block, (xs.reshape(n_blocks, MOE_BLOCK, d), block_e)).reshape(rows, d)
    contrib = (ys[dest] * sw[:, None]).astype(h.dtype)
    out = jnp.zeros((m, d), h.dtype).at[stok].add(contrib)
    return out.reshape(bsz, seq, d)

def second_inputs(seed: int = 0) -> dict:
    key = jax.random.key(seed)
    ks = jax.random.split(key, 32)
    nrm = jax.random.normal
    uni = jax.random.uniform
    f32 = jnp.float32
    dt0 = jnp.exp(uni(ks[8], (DEPTH, SSD_HEADS), f32, np.log(1e-3), np.log(1e-1)))
    return {
        'x': nrm(ks[0], (BATCH, SEQ, D_MODEL), f32),
        'c': nrm(ks[1], (BATCH, D_MODEL), f32),
        'ada_w': nrm(ks[2], (DEPTH, D_MODEL, 6 * D_MODEL), f32) * (0.5 * D_MODEL ** -0.5),
        'ada_b': 0.02 * nrm(ks[3], (DEPTH, 6 * D_MODEL), f32),
        'norm_mix_g': 1.0 + 0.02 * nrm(ks[4], (DEPTH, D_MODEL), f32),
        'w_in': nrm(ks[5], (DEPTH, D_MODEL, D_IN_2), f32) * D_MODEL ** -0.5,
        'ssd_conv_w': nrm(ks[6], (DEPTH, SSD_CONV, XBC_WIDTH), f32) * SSD_CONV ** -0.5,
        'ssd_conv_b': 0.02 * nrm(ks[7], (DEPTH, XBC_WIDTH), f32),
        'ssd_dt_bias': dt0 + jnp.log(-jnp.expm1(-dt0)),
        'ssd_a_log': jnp.log(uni(ks[9], (DEPTH, SSD_HEADS), f32, 1.0, 16.0)),
        'ssd_d': 1.0 + 0.02 * nrm(ks[10], (DEPTH, SSD_HEADS), f32),
        'ssd_norm_g': 1.0 + 0.02 * nrm(ks[11], (DEPTH, SSD_WIDTH), f32),
        'fox_f_bias': uni(ks[12], (DEPTH, ATTN_HEADS), f32, 1.0, 4.0),
        'fox_norm_g': 1.0 + 0.02 * nrm(ks[13], (DEPTH, ATTN_WIDTH), f32),
        'cm_conv_w': nrm(ks[14], (DEPTH, CONV_KERNEL, CONV_WIDTH), f32) * CONV_KERNEL ** -0.5,
        'cm_conv_b': 0.02 * nrm(ks[15], (DEPTH, CONV_WIDTH), f32),
        'cm_ln_g': 1.0 + 0.02 * nrm(ks[16], (DEPTH, CONV_WIDTH), f32),
        'cm_ln_b': 0.02 * nrm(ks[17], (DEPTH, CONV_WIDTH), f32),
        'w_out': nrm(ks[18], (DEPTH, D_MIX_2, D_MODEL), f32) * D_MIX_2 ** -0.5,
        'norm_ffn_g': 1.0 + 0.02 * nrm(ks[19], (DEPTH, D_MODEL), f32),
        'w_router_group': nrm(ks[20], (DEPTH, D_MODEL, N_EXPERT_GROUPS), f32) * D_MODEL ** -0.5,
        'b_router_group': 0.01 * nrm(ks[21], (DEPTH, N_EXPERT_GROUPS), f32),
        'w_router_expert': nrm(ks[22], (DEPTH, D_MODEL, N_EXPERTS), f32) * D_MODEL ** -0.5,
        'b_router_expert': 0.01 * nrm(ks[23], (DEPTH, N_EXPERTS), f32),
        'w_gate': nrm(ks[24], (DEPTH, N_EXPERTS, D_MODEL, D_EXPERT), f32) * D_MODEL ** -0.5,
        'w_up': nrm(ks[25], (DEPTH, N_EXPERTS, D_MODEL, D_EXPERT), f32) * D_MODEL ** -0.5,
        'w_down': nrm(ks[26], (DEPTH, N_EXPERTS, D_EXPERT, D_MODEL), f32) * D_EXPERT ** -0.5,
        'final_norm_g': 1.0 + 0.02 * nrm(ks[27], (D_MODEL,), f32),
    }

def second_block(x, c, ada_w, ada_b, norm_mix_g, w_in, ssd_conv_w, ssd_conv_b, ssd_dt_bias,
              ssd_a_log, ssd_d, ssd_norm_g, fox_f_bias, fox_norm_g, cm_conv_w, cm_conv_b,
              cm_ln_g, cm_ln_b, w_out, norm_ffn_g, w_router_group, b_router_group,
              w_router_expert, b_router_expert, w_gate, w_up, w_down, final_norm_g):
    cond = jax.nn.silu(c)
    for l in range(DEPTH):
        mod = (cond @ ada_w[l] + ada_b[l])[:, None, :]
        sh_m, sc_m, g_m, sh_f, sc_f, g_f = jnp.split(mod, 6, axis=-1)
        h = rms_norm_2(x, norm_mix_g[l]) * (1.0 + sc_m) + sh_m
        y = hybrid_mixer(h, w_in[l], ssd_conv_w[l], ssd_conv_b[l], ssd_dt_bias[l], ssd_a_log[l],
                         ssd_d[l], ssd_norm_g[l], fox_f_bias[l], fox_norm_g[l], cm_conv_w[l],
                         cm_conv_b[l], cm_ln_g[l], cm_ln_b[l], w_out[l])
        x = x + g_m * y
        h = rms_norm_2(x, norm_ffn_g[l]) * (1.0 + sc_f) + sh_f
        y = hierarchical_moe(h, w_router_group[l], b_router_group[l], w_router_expert[l],
                             b_router_expert[l], w_gate[l], w_up[l], w_down[l])
        x = x + g_f * y
    return rms_norm_2(x, final_norm_g)


def setup_inputs(seed=0):
    out = dict(first_inputs(seed))
    for name, value in second_inputs(seed + 1).items():
        if name != "x":
            out[name + "_2"] = value
    return out


def reference(
    x, c, norm_g, w_ada, b_ada, w_in, mu_shift, w0, w2, a0, a2, k_k, k_a, r_k, lnx_g, lnx_b,
    q_norm_g, k_norm_g, rel_bias, w_out, c_2, ada_w_2, ada_b_2, norm_mix_g_2, w_in_2,
    ssd_conv_w_2, ssd_conv_b_2, ssd_dt_bias_2, ssd_a_log_2, ssd_d_2, ssd_norm_g_2, fox_f_bias_2,
    fox_norm_g_2, cm_conv_w_2, cm_conv_b_2, cm_ln_g_2, cm_ln_b_2, w_out_2, norm_ffn_g_2,
    w_router_group_2, b_router_group_2, w_router_expert_2, b_router_expert_2, w_gate_2, w_up_2,
    w_down_2, final_norm_g_2,
):
    x = first_block(
        x, c, norm_g, w_ada, b_ada, w_in, mu_shift, w0, w2, a0, a2, k_k, k_a, r_k, lnx_g, lnx_b,
        q_norm_g, k_norm_g, rel_bias, w_out,
    )
    return second_block(
        x, c_2, ada_w_2, ada_b_2, norm_mix_g_2, w_in_2, ssd_conv_w_2, ssd_conv_b_2,
        ssd_dt_bias_2, ssd_a_log_2, ssd_d_2, ssd_norm_g_2, fox_f_bias_2, fox_norm_g_2,
        cm_conv_w_2, cm_conv_b_2, cm_ln_g_2, cm_ln_b_2, w_out_2, norm_ffn_g_2, w_router_group_2,
        b_router_group_2, w_router_expert_2, b_router_expert_2, w_gate_2, w_up_2, w_down_2,
        final_norm_g_2,
    )


_drawn_inputs = setup_inputs


def setup_inputs(seed=0):
    import zlib

    import numpy as np

    out = dict(_drawn_inputs(seed))
    spreads = {}
    factors = {'b_ada': 3.905,
     'w2': 4.417,
     'k_k': 8.0,
     'k_a': 5.31,
     'lnx_g': 4.336,
     'lnx_b': 8.0,
     'q_norm_g': 8.0,
     'k_norm_g': 8.0,
     'rel_bias': 5.151,
     'norm_mix_g_2': 6.496,
     'ssd_conv_b_2': 7.637,
     'ssd_d_2': 200.0,
     'ssd_norm_g_2': 7.919,
     'fox_f_bias_2': 3.531,
     'fox_norm_g_2': 8.0,
     'cm_conv_b_2': 8.0,
     'cm_ln_g_2': 8.0,
     'cm_ln_b_2': 8.0,
     'norm_ffn_g_2': 5.35,
     'b_router_group_2': 8.0,
     'b_router_expert_2': 8.0,
     'final_norm_g_2': 22.637}
    for name, (base, spread) in spreads.items():
        noise = np.random.default_rng([zlib.crc32(name.encode()), seed]).standard_normal(out[name].shape)
        drawn = base * np.exp(spread * noise) if base else spread * noise
        out[name] = jnp.asarray(drawn.astype(out[name].dtype))
    for name, factor in factors.items():
        out[name] = (out[name] * factor).astype(out[name].dtype)
    return out
```

```python
import concourse.bass as bass
from concourse import mybir
from contextlib import ExitStack

P = 128
SEQ, DM = 512, 1024
TT = SEQ // P
KD = DM // P
HD = 64
PAIRS = 4
D_RWKV = 512
N_REL = 192
REL_CLIP, REL_BACK = 128, 63
LEVELS = 7
CONV_K, SSD_K = 31, 4
NE, FE = 32, 512
MT = 64
NOV = 16
NEG = -1.0e30
RMS_EPS, GN_EPS = 1e-6, 64e-5

COLS = [("c", KD), ("c_2", KD), ("norm_g", KD), ("norm_mix_g_2", KD), ("norm_ffn_g_2", KD),
        ("mu_shift", 17), ("w0", 4), ("a0", 4), ("k_k", 4), ("k_a", 4), ("r_k", 4),
        ("lnx_g", 4), ("lnx_b", 4), ("q_norm_g", 1), ("k_norm_g", 1),
        ("ssd_conv_w_2", 8 * SSD_K), ("ssd_conv_b_2", 8), ("ssd_d_2", 4), ("ssd_norm_g_2", 4),
        ("fox_norm_g_2", 2), ("cm_conv_w_2", 2 * CONV_K), ("cm_conv_b_2", 2), ("cm_ln_g_2", 2),
        ("cm_ln_b_2", 2), ("dtf_bias", 1), ("ssd_a_log_2", 1)]
COL_AT, _n = {}, 0
for _name, _w in COLS:
    COL_AT[_name] = _n
    _n += _w
NCOLS = _n


def pack_columns(inputs):
    import numpy as np
    out = np.zeros((P, NCOLS), np.float32)
    for name, w in COLS:
        at = COL_AT[name]
        if name == "dtf_bias":
            out[0:8, at] = np.asarray(inputs["ssd_dt_bias_2"]).reshape(8)
            out[8:12, at] = np.asarray(inputs["fox_f_bias_2"]).reshape(4)
            continue
        a = np.asarray(inputs[name])
        if name in ("c", "c_2", "norm_g", "norm_mix_g_2", "norm_ffn_g_2"):
            out[:, at:at + w] = a.reshape(P, KD)
        elif name in ("q_norm_g", "k_norm_g"):
            out[:, at] = np.tile(a.reshape(HD), 2)
        elif name in ("ssd_conv_w_2", "cm_conv_w_2"):
            taps, ch = a.shape[1:]
            out[:, at:at + w] = a[0].reshape(taps, ch // P, P).transpose(2, 1, 0).reshape(P, w)
        elif name == "ssd_d_2":
            out[:, at:at + w] = np.repeat(a.reshape(8), HD).reshape(w, P).T
        elif name == "ssd_a_log_2":
            out[:a.size, at] = a.reshape(-1)
        else:
            out[:, at:at + w] = a.reshape(w, P).T
    return out


def build_program(nc, A):
    fp32, i32, u32 = mybir.dt.float32, mybir.dt.int32, mybir.dt.uint32
    ALU, ACT, AX = mybir.AluOpType, mybir.ActivationFunctionType, mybir.AxisListType
    MUL, ADD, SUB, MAX, MIN = ALU.mult, ALU.add, ALU.subtract, ALU.max, ALU.min
    V, S, G, T = nc.vector, nc.scalar, nc.gpsimd, nc.tensor
    ctx = ExitStack()
    with ctx:
        def sb(name, shape, dt=fp32):
            return ctx.enter_context(nc.sbuf_tensor(name, shape, dt))

        def sem(name):
            return ctx.enter_context(nc.semaphore(name))

        X = sb("X", [P, TT, DM])
        hT = sb("hT", [P, KD, SEQ])
        yT = sb("yT", [P, KD, SEQ])
        cols = sb("cols", [P, NCOLS])
        ident, ones, head_ones = (sb(n, [P, P]) for n in ("ident", "ones", "head_ones"))
        tri = sb("tri", [P, 2, P])
        small = sb("small", [P, 176])
        arena = sb("arena", [P, 36864])

        class Arena:
            def __init__(self, at=0):
                self.at = at

            def take(self, *shape):
                n = 1
                for d in shape:
                    n *= d
                assert self.at + n <= 36864, (self.at, n)
                a = arena[:, self.at:self.at + n]
                self.at += n
                if len(shape) == 2:
                    a = a.rearrange("p (a b) -> p a b", b=shape[1])
                elif len(shape) == 3:
                    a = a.rearrange("p (a b c) -> p a b c", b=shape[1], c=shape[2])
                return a

        def col(name, k=0):
            return cols[:, COL_AT[name] + k:COL_AT[name] + k + 1]

        small_at = [0]

        def tiny(n=1):
            a = small[:, small_at[0]:small_at[0] + n]
            small_at[0] += n
            assert small_at[0] <= 176
            return a

        banks = [ctx.enter_context(nc.psum_tensor(f"bank{i}", [P, 512], fp32)) for i in range(8)]

        fills, fill_at = [], {}
        AHEAD = 2
        APROJ_AT, QK_AT, QK_END = (0, 1, 3), 2, 3

        def plan(name, by):
            fill_at[name] = len(fills)
            fills.append((name, by))

        def plan_proj(p, j):
            plan(("proj", p, j), "act")

        for g in range(2):
            plan(("ada", g), "dve")
        for k in range(KD):
            plan(("hT", 0, k), "dve")
        plan(("wa",), "act")
        for j in range(4):
            plan_proj(0, j)
        for p in range(PAIRS):
            plan(("zw", p), "act")
            plan(("za", p), "act")
            plan(("kk", p), "dve")
            if p == 3:
                for n in range(2):
                    plan(("va", n), "act")
            if p < 3:
                plan(("ada", 2 + p), "dve")
            plan(("bonus", p), "dve")
            for c in range(TT):
                plan(("tok", p, c), "act")
            for h in range(2):
                for j in range(5):
                    plan(("gram", p, h, j), "dve")
            for l in range(1, LEVELS):
                for h in range(2):
                    plan(("W", p, l, h), "act")
                if l <= 4 and p + 1 < PAIRS:
                    plan_proj(p + 1, l - 1)
                if l <= 2 and p == 3:
                    plan(("va", l + 1), "act")
                for h in range(2):
                    if l < LEVELS - 1:
                        plan(("D", p, l, h), "dve")
                    plan(("DT", p, l, h), "dve")
            plan(("akv", p), "act")
            plan(("TaT", p), "act")
            for c in range(TT):
                plan(("U", p, c), "act")
                if c + 1 < TT:
                    plan(("S", p, c), "dve")
            plan(("Y", p), "act")
            plan(("mean", p), "dve")
            plan(("var", p), "act")
        def plan_qk(p):
            plan(("qn", p), "act")
            plan(("kn", p), "act")

        for j in range(3):
            plan(("aproj", 0, j), "act")
        plan_qk(0)
        for p in range(PAIRS):
            for i in range(AHEAD):
                plan(("score", p, i), "dve")
            for i in range(2 * TT):
                if i + AHEAD < 2 * TT:
                    plan(("score", p, i + AHEAD), "dve")
                plan(("PT", p, i), "act")
                if p + 1 < PAIRS:
                    if i in APROJ_AT:
                        plan(("aproj", p + 1, APROJ_AT.index(i)), "act")
                    if i == QK_AT:
                        plan_qk(p + 1)
                if i:
                    plan(("O", p, i - 1), "dve")
            plan(("O", p, 2 * TT - 1), "dve")
        for n in range(8):
            plan(("out", 0, n), "dve")
        for k in range(KD):
            plan(("hT", 1, k), "dve")
        plan(("dtf",), "dve")
        for i in range(2):
            plan(("glu_a", i), "act")
            plan(("glu_b", i), "act")
        for i in range(2):
            plan(("fq", i), "act")
        for i in range(2):
            plan(("fk", i), "act")
        for i in range(2):
            plan(("fv", i), "act")
        plan(("dtf_tok",), "act")
        for i in range(8):
            plan(("xbc", i), "act")
        for h in range(4):
            plan(("cumk", h), "dve")
        for i in range(AHEAD):
            plan(("fs", i), "dve")
        for i in range(4 * TT):
            if i + AHEAD < 4 * TT:
                plan(("fs", i + AHEAD), "dve")
            plan(("fPT", i), "act")
            if i:
                plan(("fO", i - 1), "act")
        plan(("fO", 4 * TT - 1), "act")
        plan(("fnorm",), "act")
        plan(("cmean",), "dve")
        plan(("cvar",), "act")
        for i in range(4):
            plan(("z", i), "act")
        plan(("alast",), "dve")
        for g in range(2):
            plan(("cb", g), "dve")
        for c in range(TT):
            plan(("xtok", c), "dve")
        for i in range(2):
            plan(("btok", i), "act")
        for c in range(TT - 1):
            plan(("st", c), "dve")
        for h in range(8):
            plan(("acs", h), "act")
            if h % 2:
                plan(("ys", h // 2), "dve")
        for g in range(2):
            plan(("snorm", g), "act")
        for n in range(8):
            plan(("out", 1, n), "dve")
        for k in range(KD):
            plan(("hT", 2, k), "dve")
        plan(("logits",), "dve")
        plan(("rank",), "dve")
        plan(("slots",), "dve")

        given = {"act": {}, "dve": {}}
        for name, by in fills:
            given[by][name] = len(given[by]) + 1
        filled = sem("psum_filled")
        emptied = {"act": sem("psum_emptied_by_act"), "dve": sem("psum_emptied_by_dve")}
        pe_next, empty_next = [0], {"act": [1], "dve": [1]}

        class Own:
            def __init__(self, eng, name):
                self.eng, self.sem, self.n = eng, sem(name), 0

            def done(self, ins):
                self.n += 1
                ins.then_inc(self.sem, 1)
                self.eng.wait_ge(self.sem, self.n)

        def fill(name):
            n = pe_next[0]
            assert fills[n][0] == name, (fills[n], name)
            if n >= 8:
                old, by = fills[n - 8]
                T.wait_ge(emptied[by], given[by][old])
            return banks[n % 8]

        def full(ins):
            ins.then_inc(filled, 1)
            pe_next[0] += 1

        def take(eng, name):
            eng.wait_ge(filled, fill_at[name] + 1)
            return banks[fill_at[name] % 8]

        def empty(eng, by, ins, name):
            assert given[by][name] == empty_next[by][0], name
            empty_next[by][0] += 1
            ins.then_inc(emptied[by], 1)
            eng.wait_ge(emptied[by], given[by][name])

        def wait_emptied(eng, name):
            by = fills[fill_at[name]][1]
            eng.wait_ge(emptied[by], given[by][name])

        NRING = 4
        RING_AT = 36864 - NRING * KD * P
        ring = Arena(RING_AT).take(NRING, KD, P)
        a1 = Arena()
        ada_ring = a1.take(2, 2048)
        level_up = a1.take(LEVELS, P)
        level_lo = a1.take(P)
        scan_mask = a1.take(SEQ)
        phase = Arena(a1.at)
        raw = phase.take(4, 514)
        sh = phase.take(4, SEQ)
        TW = phase.take(SEQ)
        w2sb = phase.take(D_RWKV)
        t_ld, t_cum, t_exc, t_dec, t_inv, t_a, t_rn, t_kk, t_k2, t_b, t_bonus = (
            phase.take(SEQ) for _ in range(11))
        alr = phase.take(TT, 2, P)
        bpad = phase.take(2, SEQ)
        kpad = phase.take(2, SEQ)
        tok = phase.take(TT, 4, P)
        mod_row = phase.take(SEQ)
        ada_bias = phase.take(SEQ)
        LbT = phase.take(8, 2, P)
        LkT = phase.take(8, 2, P)
        Dm, DmT, Wm, Lf = (phase.take(8, P) for _ in range(4))
        akv = phase.take(TT, 2, HD)
        TaT = phase.take(TT, P)
        Ut = phase.take(TT, P)
        Sb = phase.take(3, P)
        t_g, t_y = t_exc, t_inv

        cact = tiny(2 * KD)
        cactB = sb("cactB", [P, 2 * KD, 32])
        negw0, nega0, omka, kk1024 = tiny(4), tiny(4), tiny(4), tiny(4)
        modc = [tiny(KD) for _ in range(6)]
        AB = [tiny(KD) for _ in range(3)]
        ss, rstd = tiny(TT), tiny(TT)
        midf, endf = tiny(4), tiny(4)
        fcol = tiny(4)
        eps_rms, eps_gn, ln2c = tiny(1), tiny(1), tiny(1)
        qg8 = tiny(1)
        nmx, rsum, rrec = tiny(4), tiny(4), tiny(4)

        dve, act, pool = (Own(e, n) for e, n in
                          ((V, "dve_own"), (S, "act_own"), (G, "pool_own")))
        s_cols, s_x, s_small, s_adaw = (sem(n) for n in (
            "cols_loaded", "x_loaded", "small_weights_loaded", "ada_bias_loaded"))
        s_const = sem("constants_made")
        s_cact = sem("c_activated")
        s_modst, s_modld = sem("mod_stored"), sem("mod_loaded")
        s_mod = sem("mod_rows_made")
        s_xn = sem("xn_made")
        s_shift, s_ld, s_dec, s_exps = (sem(n) for n in (
            "shifted", "logdecay_exp_made", "decays_made", "exponentials_made"))
        s_sq, s_rn_in, s_rn, s_ops, s_bk = (sem(n) for n in (
            "k_squared", "norm_ready_for_ln", "norm_made", "operands_made", "bonus_operand_made"))
        s_lf = sem("level_masked")
        s_pair = sem("pair_out")
        s_yc, s_yg = sem("centered"), sem("gate_exp_made")
        s_tw = sem("lora_inputs_shifted")
        s_biasrow, s_biasst, s_biasld = sem("bias_rows_made"), sem("bias_rows_stored"), sem("bias_loaded")
        s_bias = sem("bias_masked")
        s_gateB = sem("gate_loaded")
        s_out = sem("out_stored")

        mod_dram = nc.dram_tensor("mod_scratch", [9 * DM], fp32, kind="Internal").ap()
        y_dram = nc.dram_tensor("expert_rows", [(NE + NOV) * MT, DM], fp32, kind="Internal").ap()
        s_zero = sem("extra_rows_zeroed")
        ERL = 127 + 512
        er_dram = nc.dram_tensor("bias_scratch", [8, P, ERL], fp32, kind="Internal").ap()

        ph2 = Arena()
        va = ph2.take(TT, 512)
        er = ph2.take(ERL + 1)
        bias = ph2.take(8, 512)
        aq = ph2.take(3, SEQ)
        asq = ph2.take(2, SEQ)
        qpads = [ph2.take(2, SEQ) for _ in range(2)]
        kns = ph2.take(2, SEQ)
        sc = ph2.take(4, SEQ)
        PTs = ph2.take(2, SEQ)
        gateB = ph2.take(DM)
        aegs = ph2.take(2, SEQ)
        assert phase.at <= RING_AT and ph2.at <= RING_AT

        w_in_v = A["w_in"].rearrange("(p k) n -> p k n", k=KD)
        w_out_v = A["w_out"].rearrange("(k p) n -> p k n", p=P)
        chunks = [(w_in_v, 4 * D_RWKV)]
        chunk_fill = [("wa",)]

        def add_chunk(v, at, name, w=P):
            chunks.append((v, at) if w == P else (v, at, w))
            chunk_fill.append(name)

        for p in range(PAIRS):
            for j in range(4):
                add_chunk(w_in_v, j * D_RWKV + p * P, ("proj", p, j))
        AT0 = 4 * D_RWKV + 128
        for n in range(4):
            add_chunk(w_in_v, AT0 + 2 * 512 + n * P, ("va", n))
        for p in range(PAIRS):
            for j, o in enumerate((0, 512, 1536)):
                add_chunk(w_in_v, AT0 + o + p * P, ("aproj", p, j))
        for n in range(8):
            add_chunk(w_out_v, n * P, ("out", 0, n))
        w_in2_v = A["w_in_2"].rearrange("(p k) n -> p k n", k=KD)
        w_out2_v = A["w_out_2"].rearrange("(k p) n -> p k n", p=P)
        Z0, XBC0, FQ0, FK0, FV0, GA0, GB0 = 0, 512, 1544, 1800, 2056, 2316, 2572
        add_chunk(A["w_dtf"].rearrange("(p k) n -> p k n", k=KD), 0, ("dtf",), 12)
        for i in range(2):
            add_chunk(w_in2_v, GA0 + i * P, ("glu_a", i))
            add_chunk(w_in2_v, GB0 + i * P, ("glu_b", i))
        for name, at in (("fq", FQ0), ("fk", FK0), ("fv", FV0)):
            for i in range(2):
                add_chunk(w_in2_v, at + i * P, (name, i))
        for i in range(8):
            add_chunk(w_in2_v, XBC0 + i * P, ("xbc", i))
        for i in range(4):
            add_chunk(w_in2_v, Z0 + i * P, ("z", i))
        for n in range(8):
            add_chunk(w_out2_v, n * P, ("out", 1, n))
        chunk_no = {name: n for n, name in enumerate(chunk_fill)}

        def chunk_ready(name):
            n = chunk_no[name]
            T.wait_ge(ring_sem[n % NRING], 16 * (n // NRING + 1))
            return ring[:, n % NRING]

        ring_sem = [sem(f"chunk_loaded_{i}") for i in range(NRING)]
        ada_sem = [sem(f"ada_loaded_{i}") for i in range(4)]
        ada_slots = [ada_ring[:, 0, :], ada_ring[:, 1, :], LbT.rearrange("p m a t -> p (m a t)"),
                     LkT.rearrange("p m a t -> p (m a t)")]

        def ada_slot(n):
            return (n % 4, n // 4) if n < 2 * KD else (n % 2, (n - 2 * KD) // 2 + 2 * KD // 4)
        s_ada_used = sem("ada_chunk_used")

        xn = yT[:, :, :].rearrange("p k t -> p (k t)").rearrange("p (t d) -> p t d", d=DM)
        ada_groups = [("w_ada", 0, 4, 0), ("w_ada", 4, 2, 0),
                      ("ada_w_2", 0, 4, KD), ("ada_w_2", 4, 4, KD), ("ada_w_2", 8, 4, KD)]
        b3 = lambda a, n=P: a.rearrange("p (c t) -> p c t", t=n)
        CH = lambda c: slice(c * P, (c + 1) * P)

        def sp_block1(sp):
            sp.dma_start(cols[:, :], A["cols"]).then_inc(s_cols, 16)
            sp.dma_start(X[:, :, :], A["x"][0].rearrange("(t p) d -> p t d", p=P)).then_inc(s_x, 16)
            ada_loads = [(g, k) for g in range(5) for k in range(KD)]
            ada_sent = [0]

            def load_ada(count):
                for _ in range(count):
                    n = ada_sent[0]
                    g, k = ada_loads[n]
                    w, at, m, _ = ada_groups[g]
                    if n >= 4:
                        sp.wait_ge(s_ada_used, n - 3 if n < 2 * KD else max(n - 1, 2 * KD))
                    sp.dma_start(ada_slots[ada_slot(n)[0]][:, 0:m * 512],
                                 A[w].rearrange("(p k) n -> p k n", k=KD)[:, k, at * 512:(at + m) * 512]
                                 ).then_inc(ada_sem[ada_slot(n)[0]], 16)
                    ada_sent[0] += 1

            load_ada(2 * KD)
            sp.dma_start(w2sb[0:64, :], A["w2"]).then_inc(s_small, 16)
            sp.dma_start(w2sb[64:128, :], A["a2"]).then_inc(s_small, 16)
            for n, name in enumerate(chunk_fill):
                c = chunks[n]
                w = c[2] if len(c) > 2 else P
                if n >= NRING:
                    sp.wait_ge(filled, fill_at[chunk_fill[n - NRING]] + 1)
                if w == P:
                    sp.dma_start(ring[:, n % NRING], c[0][:, :, c[1]:c[1] + P]).then_inc(ring_sem[n % NRING], 16)
                else:
                    with nc.allow_non_contiguous_dma(reason="a few columns"):
                        sp.dma_start(ring[:, n % NRING, :, 0:w], c[0][:, :, c[1]:c[1] + w]).then_inc(ring_sem[n % NRING], 16)
                if name in ada_after:
                    load_ada(KD)
            assert ada_sent[0] == len(ada_loads)

        ada_after = {("proj", 1, 3): 1, ("proj", 2, 3): 1, ("proj", 3, 3): 1}

        def pool_block1(eng):
            done = pool.done
            done(G.memset(ones[:, :], 1.0))
            done(G.memset(ident[:, :], 0.0))
            done(G.memset(head_ones[:, :], 0.0))
            done(G.memset(level_up.rearrange("p l t -> p (l t)"), 0.0))
            done(G.memset(level_lo, 0.0))
            done(G.memset(tri[:, :, :], 1.0))
            done(G.memset(scan_mask, 1.0))
            done(G.memset(eps_rms, RMS_EPS))
            done(G.memset(eps_gn, GN_EPS))
            done(G.memset(raw[:, :, 0:1], 0.0))
            done(G.memset(bpad.rearrange("p h t -> p (h t)"), 0.0))
            done(G.memset(kpad.rearrange("p h t -> p (h t)"), 0.0))
            done(G.memset(scan_mask.rearrange("p (c t) -> p c t", t=P)[:, :, 0:1], 0.0))
            done(G.memset(head_ones[0:64, 0:64], 1.0))
            done(G.memset(head_ones[64:128, 64:128], 1.0))
            done(G.affine_select(out=ident[:, :], in_=ident[:, :], compare_op=ALU.not_equal, fill=1.0,
                                 base=0, pattern=[[-1, P]], channel_multiplier=1))
            for i, op in enumerate((ALU.is_gt, ALU.is_ge)):
                done(G.affine_select(out=tri[:, i, :], in_=tri[:, i, :], compare_op=op, fill=0.0,
                                     base=0, pattern=[[1, P]], channel_multiplier=-1))
            for l in range(LEVELS):
                B = 1 << l
                nb = P // (2 * B)
                v = level_up[:, l, :].rearrange("p (n h b) -> p n h b", h=2, b=B)[:, :, 1, :]
                done(G.memset(v, 1.0))
                done(G.affine_select(out=v, in_=v, compare_op=ALU.is_ge, fill=0.0, base=0,
                                     pattern=[[-2 * B, nb], [0, B]], channel_multiplier=1))
                done(G.affine_select(out=v, in_=v, compare_op=ALU.is_ge, fill=0.0, base=B - 1,
                                     pattern=[[2 * B, nb], [0, B]], channel_multiplier=-1))
            v = level_lo.rearrange("p (n h) -> p n h", h=2)[:, :, 0:1]
            done(G.memset(v, 1.0))
            done(G.affine_select(out=v, in_=v, compare_op=ALU.is_equal, fill=0.0, base=-1,
                                 pattern=[[-2, P // 2], [0, 1]], channel_multiplier=1))
            eng.sem_inc(s_const, 1)

            def bias_load(g):
                w, at, m, _ = ada_groups[g]
                b = A["b_ada" if w == "w_ada" else "ada_b_2"]
                if g:
                    wait_emptied(eng, ("ada", g - 1))
                src = bass.AP(b.tensor, at * 512, [[512, m], [0, 32], [1, 512]])
                eng.dma_start(ada_bias[0:32 * m, :], src).then_inc(s_adaw, 16)

            def mod_io(g):
                w, at, m, _ = ada_groups[g]
                base = (0 if w == "w_ada" else 3 * DM) + at * 512
                eng.wait_ge(s_mod, g + 1)
                eng.dma_start(mod_dram[base:base + m * 512].rearrange("(c n) -> c n", n=512),
                              mod_row[0:32 * m:32, :]).then_inc(s_modst, 16)
                if g + 1 < 5:
                    eng.wait_ge(s_modst, 16 * (g + 1))
                    bias_load(g + 1)

            def mod_cols(i, at):
                eng.dma_start(modc[i], mod_dram[at:at + DM].rearrange("(p k) -> p k", k=KD)).then_inc(s_modld, 16)

            bias_load(0)
            mod_io(0)
            eng.wait_ge(s_modst, 16)
            mod_cols(0, 0)
            mod_cols(1, DM)
            mod_io(1)
            eng.dma_start(y_dram[NE * MT:, :].rearrange("(p r) d -> p r d", p=P),
                          bpad.rearrange("p (o h) t -> p o (h t)", o=1).to_broadcast([P, NOV * MT // P, DM])).then_inc(s_zero, 16)
            n = 0
            for p in range(PAIRS):
                eng.wait_ge(s_ops, 2 * p + 2)
                for l in range(1, LEVELS):
                    if n:
                        eng.wait_ge(filled, fill_at[("W", p, l - 1, 1) if l > 1 else ("W", p - 1, LEVELS - 1, 1)] + 1)
                    done(G.tensor_tensor(Lf, LbT[:, :, 0, :], level_up[:, l:l + 1, :].to_broadcast([P, 8, P]), MUL))
                    eng.sem_inc(s_lf, 1)
                    n += 1
                if p < 3:
                    mod_io(2 + p)
                if p == 2:
                    eng.dma_start(er[0:8, 383:383 + N_REL], A["rel_rev"]).then_inc(s_biasrow, 16)
                    eng.wait_ge(s_biasrow, 16)
                    done(G.tensor_copy(er[0:8, 0:383], er[0:8, 383:384].to_broadcast([8, 383])))
                    done(G.tensor_copy(er[0:8, 575:ERL], er[0:8, 574:575].to_broadcast([8, ERL - 575])))
                    eng.dma_start(er_dram, er[0:8, 0:ERL].unsqueeze(1).to_broadcast([8, P, ERL])).then_inc(s_biasst, 16)
            eng.wait_ge(s_modst, 16 * 5)
            mod_cols(2, 3 * DM)
            mod_cols(3, 4 * DM)
            mod_cols(4, 6 * DM)
            mod_cols(5, 7 * DM)
            eng.wait_ge(s_pair, PAIRS)
            eng.wait_ge(s_biasst, 16)
            for h in range(8):
                src = bass.AP(er_dram.tensor, h * P * ERL + 127, [[ERL - 1, P], [1, 512]])
                eng.dma_start(bias[:, h, :], src).then_inc(s_biasld, 16)
            eng.dma_start(gateB, bass.AP(mod_dram.tensor, 2 * DM, [[0, P], [1, DM]])).then_inc(s_gateB, 16)
            eng.wait_ge(s_biasld, 16 * 8)
            done(G.memset(bias[0:64, :, 448:512], NEG))
            eng.sem_inc(s_bias, 1)

        def act_norm(i):
            for t in range(TT):
                last = S.activation(xn[:, t, :], X[:, t, :], ACT.Square, accum_out=ss[:, t:t + 1])
            act.done(last)
            act.done(S.activation(rstd, ss, ACT.Ln, scale=1.0 / DM, bias=eps_rms))
            act.done(S.activation(rstd, rstd, ACT.Exp, scale=-0.5))
            S.sem_inc(s_sq_rows, 1)

        s_sq_rows = sem("row_norms_made")

        def dve_norm(i):
            V.wait_ge(s_sq_rows, i + 1)
            for t in range(TT):
                last = V.tensor_scalar(xn[:, t, :], X[:, t, :], rstd[:, t:t + 1], None, MUL)
            dve.done(last)
            V.sem_inc(s_xn, 1)

        def dve_gain(i, gain):
            dve.done(V.scalar_tensor_tensor(AB[i], modc[2 * i + 1], 1.0,
                                            cols[:, COL_AT[gain]:COL_AT[gain] + KD], ADD, MUL))

        def pe_norm(i):
            T.wait_ge(s_xn, i + 1)
            for k in range(KD):
                bank = fill(("hT", i, k))
                for t in range(TT):
                    last = T.transpose(bank[:, CH(t)], xn[:, t, k::KD], ident[:, :])
                full(last)

        def dve_hT(i):
            for k in range(KD):
                bank = take(V, ("hT", i, k))
                empty(V, "dve", V.tensor_scalar(hT[:, k, :], bank[:, :], AB[i][:, k:k + 1],
                                                modc[2 * i][:, k:k + 1], MUL, ADD), ("hT", i, k))

        def pe_ada(g):
            w, at, m, c0 = ada_groups[g]
            bank = fill(("ada", g))
            for k in range(KD):
                n = g * KD + k
                slot, turn = ada_slot(n)
                T.wait_ge(ada_sem[slot], 16 * (turn + 1))
                for j in range(m):
                    last = T.matmul(bank[32 * j:32 * j + 32, :], cactB[:, c0 + k, :],
                                    ada_slots[slot][:, j * 512:(j + 1) * 512], start=k == 0, stop=k == KD - 1)
                if k < KD - 1:
                    last.then_inc(s_ada_used, 1)
            full(last)
            T.wait_ge(filled, pe_next[0])
            T.sem_inc(s_ada_used, 1)

        def pe_proj(name, rows=P):
            bank = fill(name)
            w = chunk_ready(name)
            for k in range(KD):
                last = T.matmul(bank[0:rows, :], w[:, k, 0:rows], hT[:, k, :], start=k == 0, stop=k == KD - 1)
            full(last)

        def pe_rows(name, src):
            bank = fill(name)
            w = chunk_ready(name)
            for t in range(TT):
                for k in range(KD):
                    last = T.matmul(bank[:, CH(t)], src[:, k, CH(t)], w[:, k, :], start=k == 0, stop=k == KD - 1)
            full(last)

        def pe_block1(eng):
            eng.wait_ge(s_const, 1)
            eng.wait_ge(s_cact, 1)
            pe_ada(0)
            pe_ada(1)
            pe_norm(0)
            wait_emptied(eng, ("hT", 0, KD - 1))
            pe_proj(("wa",))
            for j in range(4):
                pe_proj(("proj", 0, j))
            eng.wait_ge(s_small, 32)
            eng.wait_ge(s_tw, 1)
            for p in range(PAIRS):
                for name, r in ((("zw", p), 0), (("za", p), 64)):
                    full(T.matmul(fill(name)[:, :], w2sb[r:r + 64, CH(p)], TW[r:r + 64, :], start=True, stop=True))
                eng.wait_ge(s_sq, 2 * p + 1)
                full(T.matmul(fill(("kk", p))[:, :], head_ones[:, :], t_rn, start=True, stop=True))
                if p < 3:
                    pe_ada(2 + p)
                else:
                    for n in range(2):
                        pe_rows(("va", n), hT)
                eng.wait_ge(s_bk, p + 1)
                full(T.matmul(fill(("bonus", p))[:, :], head_ones[:, :], t_bonus, start=True, stop=True))
                eng.wait_ge(s_ops, 2 * p + 1)
                eng.wait_ge(s_pads, p + 1)
                for c in range(TT):
                    bank = fill(("tok", p, c))
                    for i, src in enumerate((alr[:, c, 0, :], t_b[:, CH(c)], t_k2[:, CH(c)], sh[:, 2, CH(c)])):
                        last = T.transpose(bank[:, CH(i)], src, ident[:, :])
                    full(last)
                for h in range(2):
                    bank = fill(("gram", p, h, 0))
                    for c in range(TT):
                        last = T.matmul(bank[:, CH(c)], alr[:, c, 0, :], bpad[:, h, CH(c)], start=True, stop=True)
                    full(last)
                    for j, pad in ((1, bpad), (3, kpad)):
                        for i in range(2):
                            bank = fill(("gram", p, h, j + i))
                            for u in range(2):
                                c = 2 * i + u
                                last = T.matmul(bank[:, 256 * u:256 * u + 256], pad[:, h, CH(c)],
                                                alr[:, c, :, :].rearrange("p a t -> p (a t)"), start=True, stop=True)
                            full(last)
                for l in range(1, LEVELS):
                    eng.wait_ge(s_lf, 6 * p + l)
                    for h in range(2):
                        if l == 1:
                            eng.wait_ge(s_ops, 2 * p + 2)
                        else:
                            wait_emptied(eng, ("DT", p, l - 1, h))
                        bank = fill(("W", p, l, h))
                        for c in range(TT):
                            last = T.matmul(bank[:, CH(c)], Lf[:, 4 * h + c, :], Dm[:, 4 * h + c, :], start=True, stop=True)
                        full(last)
                    if l <= 4 and p + 1 < PAIRS:
                        pe_proj(("proj", p + 1, l - 1))
                    if l <= 2 and p == 3:
                        pe_rows(("va", l + 1), hT)
                    for h in range(2):
                        wait_emptied(eng, ("W", p, l, h))
                        if l < LEVELS - 1:
                            bank = fill(("D", p, l, h))
                            for c in range(TT):
                                last = T.matmul(bank[:, CH(c)], DmT[:, 4 * h + c, :], Wm[:, 4 * h + c, :], start=True, stop=True)
                            full(last)
                        bank = fill(("DT", p, l, h))
                        for c in range(TT):
                            last = T.matmul(bank[:, CH(c)], Wm[:, 4 * h + c, :], DmT[:, 4 * h + c, :], start=True, stop=True)
                        full(last)
                bank = fill(("akv", p))
                for c in range(TT):
                    for h in range(2):
                        last = T.matmul(bank[:, (2 * c + h) * HD:(2 * c + h + 1) * HD], LkT[:, 4 * h + c, 0, :],
                                        tok[:, c, 3, h * HD:(h + 1) * HD], start=True, stop=True)
                full(last)
                wait_emptied(eng, ("DT", p, LEVELS - 1, 1))
                bank = fill(("TaT", p))
                for c in range(TT):
                    for h in range(2):
                        last = T.matmul(bank[64 * h:64 * h + 64, CH(c)], tok[:, c, 0, h * HD:(h + 1) * HD],
                                        DmT[:, 4 * h + c, :], start=True, stop=True)
                full(last)
                wait_emptied(eng, ("TaT", p))
                for c in range(TT):
                    if c:
                        wait_emptied(eng, ("S", p, c - 1))
                    bank = fill(("U", p, c))
                    for h in range(2):
                        o = bank[:, h * HD:(h + 1) * HD]
                        if c:
                            T.matmul(o, TaT[:, c, :], Sb[:, c - 1, h * HD:(h + 1) * HD], start=True, stop=False)
                        last = T.matmul(o, DmT[:, 4 * h + c, :], akv[:, c, h, :], start=not c, stop=True)
                    full(last)
                    if c + 1 < TT:
                        bank = fill(("S", p, c))
                        if c:
                            T.matmul(bank[:, 0:P], ident[:, :], Sb[:, c - 1, :], start=True, stop=False)
                        T.matmul(bank[:, 0:P], tok[:, c, 2, :], tok[:, c, 3, :], start=not c, stop=False)
                        wait_emptied(eng, ("U", p, c))
                        full(T.matmul(bank[:, 0:P], tok[:, c, 1, :], Ut[:, c, :], start=False, stop=True))
                wait_emptied(eng, ("U", p, TT - 1))
                bank = fill(("Y", p))
                for c in range(TT):
                    for h in range(2):
                        o = bank[64 * h:64 * h + 64, CH(c)]
                        hd = slice(h * HD, (h + 1) * HD)
                        if c:
                            T.matmul(o, Sb[:, c - 1, hd], alr[:, c, 1, :], start=True, stop=False)
                        T.matmul(o, Ut[:, c, hd], LbT[:, 4 * h + c, 1, :], start=not c, stop=False)
                        last = T.matmul(o, tok[:, c, 3, hd], LkT[:, 4 * h + c, 1, :], start=False, stop=True)
                full(last)
                wait_emptied(eng, ("Y", p))
                full(T.matmul(fill(("mean", p))[:, :], head_ones[:, :], t_y, start=True, stop=True))
                eng.wait_ge(s_sq, 2 * p + 2)
                full(T.matmul(fill(("var", p))[:, :], head_ones[:, :], t_rn, start=True, stop=True))
            def qk_sums(p):
                for j, n in enumerate(("qn", "kn")):
                    eng.wait_ge(s_asq, 2 * p + j + 1)
                    full(T.matmul(fill((n, p))[:, :], head_ones[:, :], asq[:, j, :], start=True, stop=True))

            def score(p, i):
                h, t = divmod(i, TT)
                n = (t + 1) * P
                full(T.matmul(fill(("score", p, i))[:, 0:n], qpads[p % 2][:, h, CH(t)], kns[:, p % 2, 0:n], start=True, stop=True))

            def out_rows(p, i):
                h, t = divmod(i, TT)
                wait_emptied(eng, ("PT", p, i))
                bank = fill(("O", p, i))
                for j in range(t + 1):
                    last = T.matmul(bank[64 * h:64 * h + 64, 0:P], va[:, j, (2 * p + h) * HD:(2 * p + h + 1) * HD],
                                    PTs[:, i % 2, CH(j)], start=j == 0, stop=j == t)
                full(last)

            for j in range(3):
                pe_proj(("aproj", 0, j))
            qk_sums(0)
            for p in range(PAIRS):
                eng.wait_ge(s_qk, p + 1)
                for i in range(AHEAD):
                    score(p, i)
                for i in range(2 * TT):
                    if i + AHEAD < 2 * TT:
                        score(p, i + AHEAD)
                    eng.wait_ge(s_prob, 8 * p + i + 1)
                    bank = fill(("PT", p, i))
                    for j in range(i % TT + 1):
                        last = T.transpose(bank[:, CH(j)], sc[:, i % 4, CH(j)], ident[:, :])
                    full(last)
                    if p + 1 < PAIRS:
                        if i in APROJ_AT:
                            pe_proj(("aproj", p + 1, APROJ_AT.index(i)))
                        if i == QK_AT:
                            qk_sums(p + 1)
                    if i:
                        out_rows(p, i - 1)
                out_rows(p, 2 * TT - 1)
            wait_emptied(eng, ("O", 3, 7))
            for n in range(8):
                pe_rows(("out", 0, n), yT)

        s_aegate = sem("attn_gate_made")
        s_pads, s_asq, s_qk, s_prob = sem("pads_made"), sem("qk_squared"), sem("qk_normed"), sem("probs_made")
        s_arn, s_smax, s_pexp = sem("qk_norm_made"), sem("score_max_made"), sem("prob_exp_made")
        s_aeg = sem("attn_gate_exp_made")
        s_pairA = sem("attn_pair_out")

        def act_block1(eng):
            S.preload_act_table_set("natural_log_exp_and_others")
            eng.wait_ge(s_cols, 16)
            act.done(S.activation(cact, cols[:, 0:2 * KD], ACT.Exp, scale=-1.0))
            eng.sem_inc(s_cact_exp, 1)
            eng.wait_ge(s_x, 16)
            eng.wait_ge(s_const, 1)
            act_norm(0)

            def proj_raw(p, j):
                if p or not j:
                    eng.wait_ge(s_shift, 1 + 4 * (p - 1) + j + 1 if p else 1)
                bank = take(S, ("proj", p, j))
                empty(S, "act", S.activation(raw[:, j, 1:513], bank[:, :], ACT.Copy), ("proj", p, j))

            def va_out(n):
                bank = take(S, ("va", n))
                empty(S, "act", S.activation(va[:, :, CH(n)], b3(bank[:, :]), ACT.Copy), ("va", n))

            bank = take(S, ("wa",))
            empty(S, "act", S.activation(raw[:, 0, 1:513], bank[:, :], ACT.Copy), ("wa",))
            for j in range(4):
                proj_raw(0, j)
            eng.wait_ge(s_tw_in, 1)
            act.done(S.activation(TW[0:64, :], TW[0:64, :], ACT.Exp, scale=2.0))
            eng.sem_inc(s_tw_exp, 1)
            for p in range(PAIRS):
                if p:
                    eng.wait_ge(s_pair, p)
                bank = take(S, ("zw", p))
                empty(S, "act", S.activation(t_ld, bank[:, :], ACT.Exp, scale=-1.0, bias=negw0[:, p:p + 1]), ("zw", p))
                bank = take(S, ("za", p))
                empty(S, "act", S.activation(t_a, bank[:, :], ACT.Exp, scale=-1.0, bias=nega0[:, p:p + 1]), ("za", p))
                eng.wait_ge(s_shift, 1 + 4 * p + 2)
                act.done(S.activation(t_rn, sh[:, 1, :], ACT.Square, scale=col("k_k", p)))
                eng.sem_inc(s_sq, 1)
                eng.wait_ge(s_rn_in, p + 1)
                act.done(S.activation(t_rn, t_rn, ACT.Ln))
                act.done(S.activation(t_rn, t_rn, ACT.Exp, scale=-0.5))
                eng.sem_inc(s_rn, 1)
                eng.wait_ge(s_dec, p + 1)
                S.activation(t_exc, t_exc, ACT.Exp)
                S.activation(fcol[:, 0:3], fcol[:, 0:3], ACT.Exp)
                S.activation(t_inv, t_cum, ACT.Exp, scale=-1.0)
                act.done(S.activation(t_cum, t_cum, ACT.Exp))
                eng.sem_inc(s_exps, 1)
                if p == 3:
                    va_out(0)
                    va_out(1)
                eng.wait_ge(s_ops, 2 * p + 1)
                if not p:
                    eng.wait_ge(s_zero, 16)
                for h, r in ((0, slice(0, 64)), (1, slice(64, 128))):
                    S.activation(bpad[r, h, :], t_b[r, :], ACT.Copy)
                    last = S.activation(kpad[r, h, :], t_k2[r, :], ACT.Copy)
                act.done(last)
                eng.sem_inc(s_pads, 1)
                for c in range(TT):
                    bank = take(S, ("tok", p, c))
                    empty(S, "act", S.activation(tok[:, c, :, :], b3(bank[:, :]), ACT.Copy), ("tok", p, c))
                for l in range(1, LEVELS):
                    for h in range(2):
                        bank = take(S, ("W", p, l, h))
                        empty(S, "act", S.activation(Wm[:, 4 * h:4 * h + 4, :], b3(bank[:, :]), ACT.Copy), ("W", p, l, h))
                    if l <= 4 and p + 1 < PAIRS:
                        proj_raw(p + 1, l - 1)
                    if l <= 2 and p == 3:
                        va_out(l + 1)
                bank = take(S, ("akv", p))
                empty(S, "act", S.activation(akv.rearrange("p c h i -> p (c h i)"), bank[:, :], ACT.Copy), ("akv", p))
                bank = take(S, ("TaT", p))
                empty(S, "act", S.activation(TaT.rearrange("p c t -> p (c t)"), bank[:, :], ACT.Copy), ("TaT", p))
                for c in range(TT):
                    bank = take(S, ("U", p, c))
                    empty(S, "act", S.activation(Ut[:, c, :], bank[:, 0:P], ACT.Copy), ("U", p, c))
                act.done(S.activation(t_g, sh[:, 3, :], ACT.Exp, scale=-1.0))
                eng.sem_inc(s_yg, 1)
                bank = take(S, ("Y", p))
                empty(S, "act", S.activation(t_y, bank[:, :], ACT.Copy), ("Y", p))
                eng.wait_ge(s_yc, p + 1)
                act.done(S.activation(t_rn, t_y, ACT.Square))
                eng.sem_inc(s_sq, 1)
                bank = take(S, ("var", p))
                empty(S, "act", S.activation(t_rn, bank[:, :], ACT.Ln, scale=1.0 / HD, bias=eps_gn), ("var", p))
                act.done(S.activation(t_rn, t_rn, ACT.Exp, scale=-0.5))
                eng.sem_inc(s_rn, 1)
            eng.wait_ge(s_pair, PAIRS)

            def aproj_out(p, j):
                name = ("aproj", p, j)
                bank = take(S, name)
                if p:
                    eng.wait_ge(s_qk, p)
                    if j == 2:
                        eng.wait_ge(s_aegate, p)
                if j < 2:
                    S.activation(aq[:, j, :], bank[:, :], ACT.Copy)
                    empty(S, "act", S.activation(asq[:, j, :], bank[:, :], ACT.Square), name)
                    eng.sem_inc(s_asq, 1)
                else:
                    S.activation(aq[:, j, :], bank[:, :], ACT.Copy)
                    if p > 1:
                        eng.wait_ge(s_pairA, p - 1)
                    empty(S, "act", S.activation(aegs[:, p % 2, :], bank[:, :], ACT.Exp, scale=-1.0), name)
                    eng.sem_inc(s_aeg, 1)

            def qk_norm(p):
                for j, n in enumerate(("qn", "kn")):
                    bank = take(S, (n, p))
                    empty(S, "act", S.activation(asq[:, j, :], bank[:, :], ACT.Ln, scale=1.0 / HD, bias=eps_rms), (n, p))
                    act.done(S.activation(asq[:, j, :], asq[:, j, :], ACT.Exp, scale=-0.5))
                    eng.sem_inc(s_arn, 1)

            def probs_exp(p, i):
                n = (i % TT + 1) * P
                eng.wait_ge(s_smax, 8 * p + i + 1)
                act.done(S.activation(sc[:, i % 4, 0:n], sc[:, i % 4, 0:n], ACT.Exp, bias=nmx[:, i % 4:i % 4 + 1],
                                      accum_out=rsum[:, i % 4:i % 4 + 1]))
                eng.sem_inc(s_pexp, 1)

            for j in range(3):
                aproj_out(0, j)
            qk_norm(0)
            for p in range(PAIRS):
                probs_exp(p, 0)
                for i in range(2 * TT):
                    n = (i % TT + 1) * P
                    if i + 1 < 2 * TT:
                        probs_exp(p, i + 1)
                    bank = take(S, ("PT", p, i))
                    empty(S, "act", S.activation(PTs[:, i % 2, 0:n], bank[:, 0:n], ACT.Copy), ("PT", p, i))
                    if p + 1 < PAIRS:
                        if i in APROJ_AT:
                            aproj_out(p + 1, APROJ_AT.index(i))
                        if i == QK_AT:
                            qk_norm(p + 1)

        s_cact_exp, s_tw_in, s_tw_exp = sem("c_exp_made"), sem("lora_ready_for_tanh"), sem("lora_exp_made")

        def silu_into(out, e, x):
            dve.done(V.tensor_scalar(e, e, 1.0, None, ADD))
            dve.done(V.reciprocal(e, e))
            dve.done(V.tensor_tensor(out, e, x, MUL))

        def dve_ada(g):
            w, at, m, _ = ada_groups[g]
            V.wait_ge(s_adaw, 16 * (g + 1))
            if g:
                V.wait_ge(s_modst, 16 * g)
            bank = take(V, ("ada", g))
            empty(V, "dve", V.tensor_tensor(mod_row[0:32 * m, :], bank[0:32 * m, :], ada_bias[0:32 * m, :], ADD), ("ada", g))
            V.sem_inc(s_mod, 1)

        def dve_block1(eng):
            eng.wait_ge(s_cols, 16)
            V.tensor_scalar(negw0, cols[:, COL_AT["w0"]:COL_AT["w0"] + 4], -1.0, None, MUL)
            V.tensor_scalar(nega0, cols[:, COL_AT["a0"]:COL_AT["a0"] + 4], -1.0, None, MUL)
            V.tensor_scalar(omka, cols[:, COL_AT["k_a"]:COL_AT["k_a"] + 4], -1.0, 1.0, MUL, ADD)
            V.tensor_scalar(kk1024, cols[:, COL_AT["k_k"]:COL_AT["k_k"] + 4], 1024.0, None, MUL)
            V.tensor_scalar(qg8, col("q_norm_g"), HD ** -0.5, None, MUL)
            eng.wait_ge(s_cact_exp, 1)
            silu_into(cact, cact, cols[:, 0:2 * KD])
            dve.done(V.tensor_copy(cactB[:, :, :], cact.rearrange("p (k m) -> p k m", m=1).to_broadcast([P, 2 * KD, 32])))
            eng.sem_inc(s_cact, 1)
            dve_norm(0)
            dve_ada(0)
            dve_ada(1)
            eng.wait_ge(s_modld, 32)
            dve_gain(0, "norm_g")
            dve_hT(0)

            def shift(name, j, out, mu):
                wait_emptied(eng, name)
                dve.done(V.tensor_tensor(out, raw[:, j, 0:512], raw[:, j, 1:513], SUB))
                dve.done(V.scalar_tensor_tensor(out, out, mu, raw[:, j, 1:513], MUL, ADD))
                eng.sem_inc(s_shift, 1)

            shift(("wa",), 0, TW, col("mu_shift", 16))
            eng.sem_inc(s_tw_in, 1)
            eng.wait_ge(s_tw_exp, 1)
            dve.done(V.tensor_scalar(TW[0:64, :], TW[0:64, :], 1.0, None, ADD))
            dve.done(V.reciprocal(TW[0:64, :], TW[0:64, :]))
            dve.done(V.tensor_scalar(TW[0:64, :], TW[0:64, :], -2.0, 1.0, MUL, ADD))
            eng.sem_inc(s_tw, 1)
            r_, k_, v_, g_ = (sh[:, j, :] for j in range(4))
            for p in range(PAIRS):
                for j in range(4):
                    shift(("proj", p, j), j, sh[:, j, :], col("mu_shift", 4 * j + p))
                wait_emptied(eng, ("za", p))
                V.tensor_scalar(t_ld, t_ld, 1.0, None, ADD)
                dve.done(V.tensor_scalar(t_a, t_a, 1.0, None, ADD))
                V.reciprocal(t_ld, t_ld)
                dve.done(V.reciprocal(t_a, t_a))
                dve.done(V.tensor_scalar(t_ld, t_ld, -(2.718281828459045 ** -0.5), None, MUL))
                eng.wait_ge(s_const, 1)
                dve.done(V.tensor_tensor_scan(t_cum, scan_mask, t_ld, 0.0, MUL, ADD))
                cum3 = b3(t_cum)
                dve.done(V.tensor_copy(midf, cum3[:, :, 63]))
                dve.done(V.tensor_tensor(cum3, cum3, midf.rearrange("p (c o) -> p c o", o=1).to_broadcast([P, TT, P]), SUB))
                V.tensor_tensor(t_exc, t_cum, t_ld, SUB)
                dve.done(V.tensor_tensor(fcol[:, 0:3], cum3[:, 0:3, P - 1], midf[:, 1:4], ADD))
                eng.sem_inc(s_dec, 1)
                bank = take(V, ("kk", p))
                empty(V, "dve", V.tensor_scalar(t_rn, bank[:, :], 1e-24, float(2 ** 20), MAX, MUL), ("kk", p))
                eng.sem_inc(s_rn_in, 1)
                dve.done(V.tensor_scalar(t_k2, t_a, col("k_a", p), omka[:, p:p + 1], MUL, ADD))
                dve.done(V.tensor_tensor(t_k2, t_k2, k_, MUL))
                dve.done(V.scalar_tensor_tensor(t_bonus, r_, col("r_k", p), t_k2, MUL, MUL))
                eng.sem_inc(s_bk, 1)
                eng.wait_ge(s_rn, 2 * p + 1)
                dve.done(V.scalar_tensor_tensor(t_kk, k_, kk1024[:, p:p + 1], t_rn, MUL, MUL))
                dve.done(V.tensor_tensor(t_b, t_kk, t_a, MUL))
                eng.wait_ge(s_exps, p + 1)
                V.scalar_tensor_tensor(alr[:, :, 0, :], b3(t_kk), -1.0, b3(t_exc), MUL, MUL)
                V.tensor_tensor(alr[:, :, 1, :], b3(r_), cum3, MUL)
                V.tensor_tensor(t_b, t_b, t_inv, MUL)
                dve.done(V.tensor_tensor(t_k2, t_k2, t_inv, MUL))
                eng.sem_inc(s_ops, 1)
                if p < 3:
                    dve_ada(2 + p)
                bank = take(V, ("bonus", p))
                empty(V, "dve", V.tensor_tensor(t_bonus, bank[:, :], v_, MUL), ("bonus", p))
                for h in range(2):
                    hs = slice(4 * h, 4 * h + 4)
                    bank = take(V, ("gram", p, h, 0))
                    empty(V, "dve", V.tensor_tensor(Dm[:, hs, :], b3(bank[:, :]),
                                                    level_lo.rearrange("p (o t) -> p o t", o=1).to_broadcast([P, TT, P]), MUL),
                          ("gram", p, h, 0))
                    dve.done(V.tensor_tensor(Dm[:, hs, :], Dm[:, hs, :], ident[:, :].rearrange("p (o t) -> p o t", o=1).to_broadcast([P, TT, P]), ADD))
                    tri2 = tri[:, :, :].rearrange("p (o a) t -> p o (a t)", o=1).to_broadcast([P, 2, 2 * P])
                    for j, dst in ((1, LbT), (3, LkT)):
                        for i in range(2):
                            bank = take(V, ("gram", p, h, j + i))
                            m = 4 * h + 2 * i
                            empty(V, "dve", V.tensor_tensor(dst[:, m:m + 2, :, :].rearrange("p m a t -> p m (a t)"),
                                                            b3(bank[:, :], 256), tri2, MUL), ("gram", p, h, j + i))
                dve.done(V.tensor_tensor(DmT, LbT[:, :, 0, :], level_up[:, 0:1, :].to_broadcast([P, 8, P]), MUL))
                dve.done(V.tensor_tensor(DmT, DmT, ident[:, :].rearrange("p (o t) -> p o t", o=1).to_broadcast([P, 8, P]), ADD))
                eng.sem_inc(s_ops, 1)
                for l in range(1, LEVELS):
                    for h in range(2):
                        hs = slice(4 * h, 4 * h + 4)
                        for n, dst in (("D", Dm), ("DT", DmT)):
                            if n == "D" and l == LEVELS - 1:
                                continue
                            bank = take(V, (n, p, l, h))
                            empty(V, "dve", V.tensor_tensor(dst[:, hs, :], b3(bank[:, :]), dst[:, hs, :], ADD), (n, p, l, h))
                for c in range(TT - 1):
                    bank = take(V, ("S", p, c))
                    empty(V, "dve", V.scalar_tensor_tensor(Sb[:, c, :], bank[:, 0:P], fcol[:, c:c + 1], head_ones[:, :], MUL, MUL),
                          ("S", p, c))
                eng.wait_ge(s_yg, p + 1)
                silu_into(t_g, t_g, g_)
                bank = take(V, ("mean", p))
                empty(V, "dve", V.scalar_tensor_tensor(t_y, bank[:, :], -1.0 / HD, t_y, MUL, ADD), ("mean", p))
                eng.sem_inc(s_yc, 1)
                eng.wait_ge(s_rn, 2 * p + 2)
                dve.done(V.scalar_tensor_tensor(t_y, t_y, col("lnx_g", p), t_rn, MUL, MUL))
                dve.done(V.scalar_tensor_tensor(t_y, t_y, col("lnx_b", p), t_bonus, ADD, ADD))
                dve.done(V.tensor_tensor(yT[:, p, :], t_y, t_g, MUL))
                eng.sem_inc(s_pair, 1)
            eng.wait_ge(s_bias, 1)
            for qpad in qpads:
                V.memset(qpad[64:128, 0, :], 0.0)
                dve.done(V.memset(qpad[0:64, 1, :], 0.0))

            def qk_normed(p):
                eng.wait_ge(s_arn, 2 * p + 2)
                for h, r in ((0, slice(0, 64)), (1, slice(64, 128))):
                    V.scalar_tensor_tensor(qpads[p % 2][r, h, :], aq[r, 0, :], qg8[r, :], asq[r, 0, :], MUL, MUL)
                dve.done(V.scalar_tensor_tensor(kns[:, p % 2, :], aq[:, 1, :], col("k_norm_g"), asq[:, 1, :], MUL, MUL))
                eng.sem_inc(s_qk, 1)

            def gate_made(p):
                eng.wait_ge(s_aeg, p + 1)
                silu_into(aegs[:, p % 2, :], aegs[:, p % 2, :], aq[:, 2, :])
                eng.sem_inc(s_aegate, 1)

            def score(p, i):
                h, t = divmod(i, TT)
                n = (t + 1) * P
                m = nmx[:, i % 4:i % 4 + 1]
                name = ("score", p, i)
                bank = take(V, name)
                empty(V, "dve", V.tensor_tensor_reduce(
                    out=sc[:, i % 4, 0:n], in0=bank[:, 0:n], in1=bias[:, 2 * p + h, 512 - n:512], scale=1.0,
                    scalar=-3.0e38, op0=ADD, op1=MAX, accum_out=m), name)
                dve.done(V.tensor_scalar(m, m, -1.0, None, MUL))
                eng.sem_inc(s_smax, 1)

            def out_rows(p, i):
                h, t = divmod(i, TT)
                bank = take(V, ("O", p, i))
                r = slice(64 * h, 64 * h + 64)
                empty(V, "dve", V.tensor_tensor(yT[r, 4 + p, CH(t)], bank[r, 0:P], aegs[r, p % 2, CH(t)], MUL), ("O", p, i))

            qk_normed(0)
            for p in range(PAIRS):
                for i in range(AHEAD):
                    score(p, i)
                for i in range(2 * TT):
                    n = (i % TT + 1) * P
                    eng.wait_ge(s_pexp, 8 * p + i + 1)
                    dve.done(V.reciprocal(rrec[:, i % 4:i % 4 + 1], rsum[:, i % 4:i % 4 + 1]))
                    dve.done(V.tensor_scalar(sc[:, i % 4, 0:n], sc[:, i % 4, 0:n], rrec[:, i % 4:i % 4 + 1], None, MUL))
                    eng.sem_inc(s_prob, 1)
                    if i + AHEAD < 2 * TT:
                        score(p, i + AHEAD)
                    if not i:
                        gate_made(p)
                    if i == QK_END and p + 1 < PAIRS:
                        qk_normed(p + 1)
                    if i:
                        out_rows(p, i - 1)
                out_rows(p, 2 * TT - 1)
                eng.sem_inc(s_pairA, 1)
            eng.wait_ge(s_gateB, 16)
            dve_out(0, gateB, asq)

        def dve_out(i, gate, tmp):
            for n in range(8):
                name = ("out", i, n)
                bank = take(V, name)
                empty(V, "dve", V.tensor_tensor(b3(tmp[:, n % 2, :]), b3(bank[:, :]),
                                                gate[:, CH(n)].rearrange("p (o t) -> p o t", o=1).to_broadcast([P, TT, P]), MUL), name)
                dve.done(V.tensor_tensor(X[:, :, CH(n)], X[:, :, CH(n)], b3(tmp[:, n % 2, :]), ADD))

        side = sb("side", [P, 2304])
        sel = side[0:12, 0:1536].rearrange("p (h m) -> p h m", m=P)
        mask12 = side[0:12, 1536:2048]
        wr = side[:, 1536:1536 + KD * 36].rearrange("p (k n) -> p k n", n=36)
        wrb = side[:, 1536 + KD * 36:1536 + KD * 36 + 36]
        last_row = side[:, 2048:2176]
        causal = side[:, 2176:2304]
        m1 = Arena()
        un = m1.take(2, 542)
        cv = m1.take(2, SEQ)
        fq = m1.take(4, SEQ)
        fk = m1.take(2, SEQ)
        fv = m1.take(TT, 256)
        ncum = m1.take(4, SEQ)
        fsc = m1.take(3, SEQ)
        fpt = m1.take(2, SEQ)
        fo = m1.take(2, SEQ)
        assert m1.at <= 12288
        m2 = Arena(12288)
        xc = m2.take(8, SEQ)
        xraw = m2.take(2, 516)
        zz = m2.take(4, SEQ)
        e0 = m2.take(2, SEQ)
        cbT = m2.take(2, SEQ)
        xdt = m2.take(TT, 512)
        xde = m2.take(2, 512)
        bmt = m2.take(TT, 2, P)
        prev = m2.take(3, 512)
        dmat = m2.take(2, SEQ)
        cms = m2.take(2, SEQ)
        tk = m2.take(TT, 2, 12)
        al = m2.take(TT, 12)
        dte = m2.take(TT, 12)
        gate2 = m2.take(DM)
        assert m2.at <= RING_AT, m2.at
        sp_x, sp_e, sp_u, sp_l = (e0[0:12, 0, :], e0[0:12, 1, :], dmat[0:12, 0, :], dmat[0:12, 1, :])
        L12 = cms[0:12, 0, :]
        AC12 = cactB[0:12, :, :].rearrange("p k m -> p (k m)")

        sgn12, mcol12 = tiny(), tiny()
        fnmx, fsum, frec = tiny(3), tiny(3), tiny(3)
        s_blk1 = sem("block1_done")
        s_const2 = sem("mixer_constants_made")
        s_sp_x, s_sp_e, s_sp_u, s_sp_l, s_ac = (sem(n) for n in (
            "softplus_abs_made", "softplus_exp_made", "softplus_sum_made", "softplus_log_made", "sums_made"))
        s_alog = sem("a_exp_made")
        s_xr, s_xconv, s_xexp, s_xc = (sem(n) for n in (
            "xraw_free", "xbc_convolved", "xbc_exp_made", "xbc_made"))
        s_fmx, s_fexp, s_fprob = sem("fox_max_made"), sem("fox_exp_made"), sem("fox_probs_made")
        s_fsq, s_frn, s_ccen, s_csq, s_crn, s_cy, s_cexp = (sem(n) for n in (
            "fox_squared", "fox_norm_made", "conv_centered", "conv_squared", "conv_norm_made",
            "conv_normed", "conv_exp_made"))
        s_conv = sem("conv_made")
        s_zexp = sem("z_exp_made")
        s_al, s_dte, s_xde = sem("chunk_sums_made"), sem("end_decays_made"), sem("xdt_decayed")
        s_prev = sem("states_made")
        s_dd, s_dexp, s_gm = sem("decay_logs_made"), sem("decay_matrix_made"), sem("ssd_operands_made")
        s_ysq_in, s_ysq, s_srn = sem("ssd_gated"), sem("ssd_squared"), sem("ssd_norm_made")
        s_gate2 = sem("gate2_loaded")

        def pool_block2(eng):
            done = pool.done
            done(G.iota(iota, pattern=[[1, 64]], base=0, channel_multiplier=0, allow_small_or_imprecise_dtypes=True))
            done(G.iota(tok1, pattern=[[P, TT]], base=1, channel_multiplier=1, allow_small_or_imprecise_dtypes=True))
            done(G.memset(causal, 0.0))
            done(G.affine_select(out=causal, in_=causal, compare_op=ALU.is_ge, fill=NEG,
                                 base=0, pattern=[[-1, P]], channel_multiplier=1))
            done(G.memset(sel[:, :, :], 0.0))
            done(G.affine_select(out=sel[:, :, :], in_=sel[:, :, :], compare_op=ALU.not_equal, fill=1.0,
                                 base=0, pattern=[[-1, 12], [0, P]], channel_multiplier=1))
            done(G.memset(mask12, 1.0))
            done(G.memset(mask12.rearrange("p (c t) -> p c t", t=P)[0:8, :, 0:1], 0.0))
            done(G.memset(last_row, 0.0))
            done(G.affine_select(out=last_row, in_=last_row, compare_op=ALU.not_equal, fill=1.0,
                                 base=-(P - 1), pattern=[[0, P]], channel_multiplier=1))
            done(G.memset(sgn12, 1.0))
            done(G.affine_select(out=sgn12, in_=sgn12, compare_op=ALU.is_gt, fill=-1.0,
                                 base=8, pattern=[[0, 1]], channel_multiplier=-1))
            eng.wait_ge(s_blk1, 1)
            done(G.memset(un[:, :, 0:30], 0.0))
            done(G.memset(xraw[:, :, 0:3], 0.0))
            for h in range(4):
                r = slice(64, 128) if h % 2 == 0 else slice(0, 64)
                done(G.memset(fq[r, h, :], 0.0))
            eng.sem_inc(s_const2, 1)
            eng.dma_start(gate2, bass.AP(mod_dram.tensor, 5 * DM, [[0, P], [1, DM]])).then_inc(s_gate2, 16)
            eng.wait_ge(s_ac, 1)
            eng.dma_start(wr, A["w_router"].rearrange("(p k) n -> p k n", k=KD)).then_inc(s_gate2, 16)
            eng.dma_start(wrb, bass.AP(A["b_router"].tensor, 0, [[0, P], [1, 36]])).then_inc(s_gate2, 16)

        def act_router(eng):
            eng.wait_ge(s_rt_in, 1)
            act.done(S.activation(r_eg, r_eg, ACT.Exp))
            eng.sem_inc(s_rt_exp, 1)
            eng.wait_ge(s_rt_in, 2)
            act.done(S.activation(r_d, r_d, ACT.Exp))
            eng.sem_inc(s_rt_exp, 1)

        def act_block2(eng):
            def copy_out(name, dst, src=None, **kw):
                bank = take(S, name)
                empty(S, "act", S.activation(dst, bank[:, :] if src is None else src(bank), kw.pop("func", ACT.Copy), **kw), name)

            eng.wait_ge(s_blk1, 1)
            act_norm(1)
            act.done(S.activation(mcol12[0:12], col("ssd_a_log_2")[0:12], ACT.Exp))
            eng.sem_inc(s_alog, 1)
            eng.wait_ge(s_sp_x, 1)
            act.done(S.activation(sp_e, sp_e, ACT.Exp, scale=-1.0))
            eng.sem_inc(s_sp_e, 1)
            eng.wait_ge(s_sp_u, 1)
            act.done(S.activation(sp_l, sp_u, ACT.Ln))
            eng.sem_inc(s_sp_l, 1)
            eng.wait_ge(s_const2, 1)
            for i in range(2):
                copy_out(("glu_a", i), un[:, i, 30:542])
                copy_out(("glu_b", i), cv[:, i, :], func=ACT.Exp, scale=-1.0)
            for i in range(2):
                bank = take(S, ("fq", i))
                S.activation(fq[0:64, 2 * i, :], bank[0:64, :], ACT.Copy, scale=HD ** -0.5)
                empty(S, "act", S.activation(fq[64:128, 2 * i + 1, :], bank[64:128, :], ACT.Copy, scale=HD ** -0.5), ("fq", i))
            for i in range(2):
                copy_out(("fk", i), fk[:, i, :])
            for i in range(2):
                copy_out(("fv", i), fv[:, :, CH(i)], lambda bank: b3(bank[:, :]))
            copy_out(("dtf_tok",), tk.rearrange("p c a h -> p (c a h)"), lambda bank: bank[:, 0:96])
            for i in range(8):
                if i >= 2:
                    eng.wait_ge(s_xr, i - 1)
                copy_out(("xbc", i), xraw[:, i % 2, 3:515])
                eng.wait_ge(s_xconv, i + 1)
                act.done(S.activation(e0[:, i % 2, :], xc[:, i, :], ACT.Exp, scale=-1.0))
                eng.sem_inc(s_xexp, 1)

            def probs_exp(i):
                n = (i % TT + 1) * P
                eng.wait_ge(s_fmx, i + 1)
                act.done(S.activation(fsc[:, i % 3, 0:n], fsc[:, i % 3, 0:n], ACT.Exp, bias=fnmx[:, i % 3:i % 3 + 1],
                                      accum_out=fsum[:, i % 3:i % 3 + 1]))
                eng.sem_inc(s_fexp, 1)

            def out_rows(i):
                h, t = divmod(i, TT)
                r = slice(64 * (h % 2), 64 * (h % 2) + 64)
                copy_out(("fO", i), fo[r, h // 2, CH(t)], lambda bank: bank[r, 0:P])

            probs_exp(0)
            for i in range(4 * TT):
                n = (i % TT + 1) * P
                if i + 1 < 4 * TT:
                    probs_exp(i + 1)
                copy_out(("fPT", i), fpt[:, i % 2, 0:n], lambda bank: bank[:, 0:n])
                if i:
                    out_rows(i - 1)
            out_rows(4 * TT - 1)
            for i in range(2):
                last = S.activation(fpt[:, i, :], fo[:, i, :], ACT.Square)
            act.done(last)
            eng.sem_inc(s_fsq, 1)
            copy_out(("fnorm",), fpt[:, 0, :], func=ACT.Ln, scale=1.0 / 256, bias=eps_rms)
            act.done(S.activation(fpt[:, 0, :], fpt[:, 0, :], ACT.Exp, scale=-0.5))
            eng.sem_inc(s_frn, 1)
            eng.wait_ge(s_ccen, 1)
            for i in range(2):
                last = S.activation(fsc[:, i, :], cv[:, i, :], ACT.Square)
            act.done(last)
            eng.sem_inc(s_csq, 1)
            copy_out(("cvar",), fsc[:, 0, :], func=ACT.Ln, scale=1.0 / 256, bias=eps_rms)
            act.done(S.activation(fsc[:, 0, :], fsc[:, 0, :], ACT.Exp, scale=-0.5))
            eng.sem_inc(s_crn, 1)
            eng.wait_ge(s_cy, 1)
            for i in range(2):
                last = S.activation(un[:, i, 0:SEQ], cv[:, i, :], ACT.Exp, scale=-1.0)
            act.done(last)
            eng.sem_inc(s_cexp, 1)
            for i in range(4):
                bank = take(S, ("z", i))
                S.activation(zz[:, i, :], bank[:, :], ACT.Copy)
                if i >= 2:
                    eng.wait_ge(s_zfree, i - 1)
                empty(S, "act", S.activation(e0[:, i % 2, :], bank[:, :], ACT.Exp, scale=-1.0), ("z", i))
                eng.sem_inc(s_zexp, 1)
            eng.wait_ge(s_al, 1)
            S.activation(dte.rearrange("p c h -> p (c h)"), dte.rearrange("p c h -> p (c h)"), ACT.Exp)
            act.done(S.activation(al.rearrange("p c h -> p (c h)"), al.rearrange("p c h -> p (c h)"), ACT.Exp))
            eng.sem_inc(s_dte, 1)
            for i in range(2):
                copy_out(("btok", i), bmt[:, 2 * i:2 * i + 2, :, :].rearrange("p c g n -> p (c g n)"))
            for h in range(8):
                eng.wait_ge(s_dd, h + 1)
                S.activation(dmat[:, h % 2, :], dmat[:, h % 2, :], ACT.Exp)
                copy_out(("acs", h), cms[:, h % 2, :], func=ACT.Exp)
                eng.sem_inc(s_dexp, 1)
            for i in range(4):
                eng.wait_ge(s_ysq_in, i + 1)
                act.done(S.activation(xdt[:, i, :], zz[:, i, :], ACT.Square))
                eng.sem_inc(s_ysq, 1)
            for g in range(2):
                copy_out(("snorm", g), e0[:, g, :], func=ACT.Ln, scale=1.0 / 256, bias=eps_rms)
                act.done(S.activation(e0[:, g, :], e0[:, g, :], ACT.Exp, scale=-0.5))
                eng.sem_inc(s_srn, 1)

        s_zfree = sem("z_gate_made")

        def pe_block2(eng):
            pe_norm(1)
            wait_emptied(eng, ("hT", 1, KD - 1))
            pe_proj(("dtf",), rows=12)
            for i in range(2):
                pe_proj(("glu_a", i))
                pe_proj(("glu_b", i))
            for n in ("fq", "fk"):
                for i in range(2):
                    pe_proj((n, i))
            for i in range(2):
                pe_rows(("fv", i), hT)
            eng.wait_ge(s_ac, 1)
            bank = fill(("dtf_tok",))
            for c in range(TT):
                for a, src in ((0, L12), (1, AC12)):
                    last = T.transpose(bank[:, (2 * c + a) * 12:(2 * c + a + 1) * 12], src[:, CH(c)], ident[0:12, 0:12])
            full(last)
            for i in range(8):
                pe_proj(("xbc", i))
            for h in range(4):
                full(T.matmul(fill(("cumk", h))[:, :], sel[:, 8 + h, :], AC12, start=True, stop=True))
            wait_emptied(eng, ("fv", 1))

            def score(i):
                h, t = divmod(i, TT)
                n = (t + 1) * P
                full(T.matmul(fill(("fs", i))[:, 0:n], fq[:, h, CH(t)], fk[:, h // 2, 0:n], start=True, stop=True))

            def out_rows(i):
                h, t = divmod(i, TT)
                wait_emptied(eng, ("fPT", i))
                bank = fill(("fO", i))
                for j in range(t + 1):
                    last = T.matmul(bank[64 * (h % 2):64 * (h % 2) + 64, 0:P], fv[:, j, h * HD:(h + 1) * HD],
                                    fpt[:, i % 2, CH(j)], start=j == 0, stop=j == t)
                full(last)

            for i in range(AHEAD):
                score(i)
            for i in range(4 * TT):
                if i + AHEAD < 4 * TT:
                    score(i + AHEAD)
                eng.wait_ge(s_fprob, i + 1)
                bank = fill(("fPT", i))
                for j in range(i % TT + 1):
                    last = T.transpose(bank[:, CH(j)], fsc[:, i % 3, CH(j)], ident[:, :])
                full(last)
                if i:
                    out_rows(i - 1)
            out_rows(4 * TT - 1)

            def both(name, src):
                bank = fill(name)
                T.matmul(bank[:, :], ones[:, :], src[0], start=True, stop=False)
                full(T.matmul(bank[:, :], ones[:, :], src[1], start=False, stop=True))
            eng.wait_ge(s_fsq, 1)
            both(("fnorm",), (fpt[:, 0, :], fpt[:, 1, :]))
            eng.wait_ge(s_conv, 1)
            both(("cmean",), (cv[:, 0, :], cv[:, 1, :]))
            eng.wait_ge(s_csq, 1)
            both(("cvar",), (fsc[:, 0, :], fsc[:, 1, :]))
            for i in range(4):
                pe_proj(("z", i))
            full(T.matmul(fill(("alast",))[:, 0:48], last_row, tk[:, :, 1, :], start=True, stop=True))
            eng.wait_ge(s_xc, 8)
            for g in range(2):
                bank = fill(("cb", g))
                for c in range(TT):
                    last = T.matmul(bank[:, CH(c)], xc[:, 4 + g, CH(c)], xc[:, 6 + g, CH(c)], start=True, stop=True)
                full(last)
            for c in range(TT):
                bank = fill(("xtok", c))
                for i in range(4):
                    last = T.transpose(bank[:, CH(i)], xc[:, i, CH(c)], ident[:, :])
                full(last)
            for i in range(2):
                bank = fill(("btok", i))
                for u in range(2):
                    for g in range(2):
                        last = T.transpose(bank[:, CH(2 * u + g)], xc[:, 4 + g, CH(2 * i + u)], ident[:, :])
                full(last)
            wait_emptied(eng, ("btok", 1))
            for c in range(TT - 1):
                eng.wait_ge(s_xde, c + 1)
                bank = fill(("st", c))
                for g in range(2):
                    last = T.matmul(bank[:, 256 * g:256 * g + 256], bmt[:, c, g, :], xde[:, c % 2, 256 * g:256 * g + 256],
                                    start=True, stop=True)
                full(last)
            for h in range(8):
                full(T.matmul(fill(("acs", h))[:, :], sel[:, h, :], AC12, start=True, stop=True))
                if h % 2 == 0:
                    continue
                eng.wait_ge(s_prev, 1)
                eng.wait_ge(s_gm, h + 1)
                bank = fill(("ys", h // 2))
                for c in range(TT):
                    for u in range(2):
                        hh = h - 1 + u
                        o = bank[64 * u:64 * u + 64, CH(c)]
                        last = T.matmul(o, xdt[:, c, hh * HD:(hh + 1) * HD], dmat[:, u, CH(c)], start=True, stop=c == 0)
                        if c:
                            last = T.matmul(o, prev[:, c - 1, hh * HD:(hh + 1) * HD], cms[:, u, CH(c)], start=False, stop=True)
                full(last)
            for g in range(2):
                eng.wait_ge(s_ysq, 2 * g + 2)
                both(("snorm", g), (xdt[:, 2 * g, :], xdt[:, 2 * g + 1, :]))
            eng.wait_ge(s_y2, 1)
            for n in range(8):
                pe_rows(("out", 1, n), yT)
            pe_norm(2)
            wait_emptied(eng, ("hT", 2, KD - 1))
            bank = fill(("logits",))
            for t in range(TT):
                for k in range(KD):
                    last = T.matmul(bank[:, 36 * t:36 * t + 36], hT[:, k, CH(t)], wr[:, k, :], start=k == 0, stop=k == KD - 1)
            full(last)
            eng.wait_ge(s_chosen, 1)
            bank = fill(("rank",))
            for t in range(TT):
                for j in range(t):
                    T.matmul(bank[:, NE * t:NE * t + NE], ones[:, :], chosen[:, j, :], start=j == 0, stop=False)
                T.matmul(bank[:, NE * t:NE * t + NE], tri[:, 0, :], chosen[:, t, :], start=not t, stop=True)
            for j in range(TT):
                last = T.matmul(bank[:, P:P + NE], ones[:, :], chosen[:, j, :], start=j == 0, stop=j == TT - 1)
            full(last)
            eng.wait_ge(s_hot, 1)
            bank = fill(("slots",))
            for n in range(2 * TT):
                last = T.matmul(bank[0:MT, 0:NE + NOV], hot_pos[:, n, :], hot_tile[:, n, :], start=n == 0, stop=n == 2 * TT - 1)
            full(last)

        s_y2, s_chosen, s_hot = sem("y2_made"), sem("experts_chosen"), sem("slots_hot")

        def dve_block2(eng):
            eng.sem_inc(s_blk1, 1)
            eng.wait_ge(s_modld, 16 * 6)
            dve_gain(1, "norm_mix_g_2")
            dve_gain(2, "norm_ffn_g_2")
            dve_norm(1)
            dve_hT(1)
            eng.wait_ge(s_const2, 1)
            bank = take(V, ("dtf",))
            empty(V, "dve", V.tensor_scalar(sp_x, bank[0:12, :], col("dtf_bias")[0:12], sgn12[0:12], ADD, MUL), ("dtf",))
            dve.done(V.scalar_tensor_tensor(sp_e, sp_x, -1.0, sp_x, MUL, MAX))
            eng.sem_inc(s_sp_x, 1)
            eng.wait_ge(s_alog, 1)
            V.tensor_scalar(mcol12[0:12], mcol12[0:12], -1.0, None, MUL)
            eng.wait_ge(s_sp_e, 1)
            dve.done(V.tensor_scalar(sp_u, sp_e, 1.0, None, ADD))
            eng.sem_inc(s_sp_u, 1)
            dve.done(V.scalar_tensor_tensor(sp_e, sp_u, -1.0, sp_e, ADD, SUB))
            eng.wait_ge(s_sp_l, 1)
            dve.done(V.reciprocal(sp_u, sp_u))
            dve.done(V.tensor_tensor(sp_e, sp_e, sp_u, MUL))
            dve.done(V.tensor_tensor(sp_l, sp_l, sp_e, SUB))
            dve.done(V.scalar_tensor_tensor(L12, sp_x, 0.0, sp_l, MAX, ADD))
            dve.done(V.tensor_scalar(sp_u, L12, mcol12[0:12], None, MUL))
            dve.done(V.tensor_tensor_scan(AC12, mask12, sp_u, 0.0, MUL, ADD))
            eng.sem_inc(s_ac, 1)
            eng.wait_ge(s_const2, 1)
            for i in range(2):
                wait_emptied(eng, ("glu_b", i))
                silu_into(un[:, i, 30:542], cv[:, i, :], un[:, i, 30:542])
            for i in range(2):
                w = lambda j: col("cm_conv_w_2", i * CONV_K + j)
                dve.done(V.tensor_scalar(cv[:, i, :], un[:, i, 30:542], w(30), col("cm_conv_b_2", i), MUL, ADD))
                for j in range(30):
                    dve.done(V.scalar_tensor_tensor(cv[:, i, :], un[:, i, j:j + SEQ], w(j), cv[:, i, :], MUL, ADD))
            eng.sem_inc(s_conv, 1)
            for i in range(8):
                wait_emptied(eng, ("xbc", i))
                w = lambda j: col("ssd_conv_w_2", i * SSD_K + j)
                dve.done(V.tensor_scalar(xc[:, i, :], xraw[:, i % 2, 3:515], w(3), col("ssd_conv_b_2", i), MUL, ADD))
                for j in range(3):
                    dve.done(V.scalar_tensor_tensor(xc[:, i, :], xraw[:, i % 2, j:j + SEQ], w(j), xc[:, i, :], MUL, ADD))
                eng.sem_inc(s_xr, 1)
                eng.sem_inc(s_xconv, 1)
                if i:
                    x_silu(eng, i - 1)
            x_silu(eng, 7)
            for h in range(4):
                bank = take(V, ("cumk", h))
                empty(V, "dve", V.tensor_scalar(ncum[:, h, :], bank[:, :], -1.0, None, MUL), ("cumk", h))

            def score(i):
                h, t = divmod(i, TT)
                n = (t + 1) * P
                s_, m = fsc[:, i % 3, 0:n], fnmx[:, i % 3:i % 3 + 1]
                bank = take(V, ("fs", i))
                empty(V, "dve", V.scalar_tensor_tensor(s_, bank[:, 0:n], tk[:, t, 1, 8 + h:9 + h], ncum[:, h, 0:n], ADD, ADD), ("fs", i))
                dve.done(V.tensor_tensor(fsc[:, i % 3, CH(t)], fsc[:, i % 3, CH(t)], causal, ADD))
                dve.done(V.reduce_max(m, s_, AX.X))
                dve.done(V.tensor_scalar(m, m, -1.0, None, MUL))
                eng.sem_inc(s_fmx, 1)

            for i in range(AHEAD):
                score(i)
            for i in range(4 * TT):
                n = (i % TT + 1) * P
                eng.wait_ge(s_fexp, i + 1)
                dve.done(V.reciprocal(frec[:, i % 3:i % 3 + 1], fsum[:, i % 3:i % 3 + 1]))
                dve.done(V.tensor_scalar(fsc[:, i % 3, 0:n], fsc[:, i % 3, 0:n], frec[:, i % 3:i % 3 + 1], None, MUL))
                eng.sem_inc(s_fprob, 1)
                if i + AHEAD < 4 * TT:
                    if i:
                        eng.wait_ge(filled, fill_at[("fPT", i - 1)] + 1)
                    score(i + AHEAD)
            eng.wait_ge(s_frn, 1)
            for i in range(2):
                dve.done(V.scalar_tensor_tensor(yT[:, 4 + i, :], fo[:, i, :], col("fox_norm_g_2", i), fpt[:, 0, :], MUL, MUL))
            bank = take(V, ("cmean",))
            V.scalar_tensor_tensor(cv[:, 0, :], bank[:, :], -1.0 / 256, cv[:, 0, :], MUL, ADD)
            empty(V, "dve", V.scalar_tensor_tensor(cv[:, 1, :], bank[:, :], -1.0 / 256, cv[:, 1, :], MUL, ADD), ("cmean",))
            eng.sem_inc(s_ccen, 1)
            eng.wait_ge(s_crn, 1)
            for i in range(2):
                dve.done(V.scalar_tensor_tensor(cv[:, i, :], cv[:, i, :], col("cm_ln_g_2", i), fsc[:, 0, :], MUL, MUL))
                dve.done(V.tensor_scalar(cv[:, i, :], cv[:, i, :], col("cm_ln_b_2", i), None, ADD))
            eng.sem_inc(s_cy, 1)
            eng.wait_ge(s_cexp, 1)
            for i in range(2):
                silu_into(yT[:, 6 + i, :], un[:, i, 0:SEQ], cv[:, i, :])
            eng.sem_inc(w_free[0], 1)
            for i in range(4):
                eng.wait_ge(s_zexp, i + 1)
                silu_into(zz[:, i, :], e0[:, i % 2, :], zz[:, i, :])
                eng.sem_inc(s_zfree, 1)
            fl = lambda a: a.rearrange("p c h -> p (c h)")
            bank = take(V, ("alast",))
            V.tensor_copy(fl(al), bank[:, 0:48])
            empty(V, "dve", V.tensor_tensor(dte, b3(bank[:, 0:48], 12), tk[:, :, 1, :], SUB), ("alast",))
            eng.sem_inc(s_al, 1)
            for g in range(2):
                bank = take(V, ("cb", g))
                empty(V, "dve", V.tensor_tensor(b3(cbT[:, g, :]), b3(bank[:, :]), tri[:, 1:2, :].to_broadcast([P, TT, P]), MUL), ("cb", g))
            per_head = lambda a: a.rearrange("p (h o) -> p h o", o=1).to_broadcast([P, 8, HD])
            for c in range(TT):
                bank = take(V, ("xtok", c))
                empty(V, "dve", V.tensor_tensor(b3(xdt[:, c, :], HD), b3(bank[:, :], HD), per_head(tk[:, c, 0, 0:8]), MUL), ("xtok", c))
            eng.wait_ge(s_dte, 1)
            for c in range(TT - 1):
                if c >= 2:
                    eng.wait_ge(filled, fill_at[("st", c - 2)] + 1)
                dve.done(V.tensor_tensor(b3(xde[:, c % 2, :], HD), b3(xdt[:, c, :], HD), per_head(dte[:, c, 0:8]), MUL))
                eng.sem_inc(s_xde, 1)
                if c:
                    state(c - 1)
            state(TT - 2)
            eng.sem_inc(s_prev, 1)
            for h in range(8):
                u, g = h % 2, h // 4
                if h >= 2:
                    eng.wait_ge(filled, fill_at[("ys", h // 2 - 1)] + 1)
                bank = take(V, ("acs", h))
                for c in range(TT):
                    last = V.tensor_scalar(dmat[:, u, CH(c)], bank[:, CH(c)], tk[:, c, 1, h:h + 1], 0.0, SUB, MIN)
                dve.done(last)
                eng.sem_inc(s_dd, 1)
                eng.wait_ge(s_dexp, h + 1)
                V.tensor_tensor(dmat[:, u, :], dmat[:, u, :], cbT[:, g, :], MUL)
                dve.done(V.tensor_tensor(cms[:, u, :], cms[:, u, :], xc[:, 6 + g, :], MUL))
                eng.sem_inc(s_gm, 1)
                if u:
                    i = h // 2
                    bank = take(V, ("ys", i))
                    empty(V, "dve", V.scalar_tensor_tensor(xc[:, i, :], xc[:, i, :], col("ssd_d_2", i), bank[:, :], MUL, ADD), ("ys", i))
                    dve.done(V.tensor_tensor(zz[:, i, :], zz[:, i, :], xc[:, i, :], MUL))
                    if i == 3:
                        for _ in range(4):
                            eng.sem_inc(s_ysq_in, 1)
            for g in range(2):
                eng.wait_ge(s_srn, g + 1)
                for i in (2 * g, 2 * g + 1):
                    dve.done(V.scalar_tensor_tensor(yT[:, i, :], zz[:, i, :], col("ssd_norm_g_2", i), e0[:, g, :], MUL, MUL))
            eng.sem_inc(s_y2, 1)
            eng.wait_ge(s_gate2, 48)
            dve_out(1, gate2, e0)
            dve_router(eng)
            dve_experts(eng)
            dve_final(eng)

        def x_silu(eng, i):
            eng.wait_ge(s_xexp, i + 1)
            silu_into(xc[:, i, :], e0[:, i % 2, :], xc[:, i, :])
            eng.sem_inc(s_xc, 1)

        def state(c):
            bank = take(V, ("st", c))
            if not c:
                empty(V, "dve", V.tensor_copy(prev[:, 0, :], bank[:, :]), ("st", 0))
                return
            dve.done(V.tensor_tensor(b3(prev[:, c, :], HD), b3(prev[:, c - 1, :], HD),
                                     al[:, c, 0:8].rearrange("p (h o) -> p h o", o=1).to_broadcast([P, 8, HD]), MUL))
            empty(V, "dve", V.tensor_tensor(prev[:, c, :], bank[:, :], prev[:, c, :], ADD), ("st", c))


        iotas = sb("iotas", [P, 68])
        iota, tok1 = iotas[:, 0:64], iotas[:, 64:68]
        rt_at = [0]

        def rt(*shape):
            n = 1
            for d in shape:
                n *= d
            a = side[:, rt_at[0]:rt_at[0] + n]
            rt_at[0] += n
            assert rt_at[0] <= 1536
            if len(shape) == 2:
                a = a.rearrange("p (a b) -> p a b", b=shape[1])
            return a

        r_lg = rt(TT, 36)
        r_ohg, r_eg = rt(TT, 4), rt(TT, 4)
        r_el, r_el2, r_oh1, r_oh2, r_cand = (rt(TT, 8) for _ in range(5))
        r_m, r_m1, r_mi, r_pg, r_d, r_w1, r_w2 = (rt(TT) for _ in range(7))
        chosen = rt(TT, NE)
        hot_pos = hT[:, 0, :].rearrange("p (n m) -> p n m", m=MT)
        hot_tile = hT[:, 1, 0:8 * (NE + NOV)].rearrange("p (n m) -> p n m", m=NE + NOV)
        r_oh = [rt(TT, NE) for _ in range(2)]
        r_rank = rt(5 * NE)
        r_nov, r_incl, r_xs = rt(NE), rt(NE), rt(NE)
        r_t = rt(TT, NE)
        r_rk, r_xk, r_ek, r_q, r_pos, r_tile = (rt(TT) for _ in range(6))
        r_v = rt(NE + NOV)
        r_ones = ones[:, 0:NE]
        dest = sb("dest", [P, 2, TT], u32)
        wts = sb("wts", [P, 2, TT])
        slots = sb("slots", [MT, NE + NOV], u32)
        ov_first = sb("ov_first", [1, NE + 1], i32)
        s_rt_in, s_rt_exp, s_routed = sem("router_ready_for_exp"), sem("router_exp_made"), sem("routed")
        s_xnst = sem("xn_stored")
        xn_dram = nc.dram_tensor("xn_scratch", [SEQ, DM], fp32, kind="Internal").ap()

        def bc(a, n):
            return a.rearrange("p (t o) -> p t o", o=1).to_broadcast([P, TT, n])

        def bt(a, n):
            return a.rearrange("p (o n) -> p o n", o=1).to_broadcast([P, TT, n])

        def dve_router(eng):
            eng.sem_inc(s_blk1, 1)
            for u in range(1, U):
                eng.sem_inc(w_free[u], 1)
            dve_norm(2)
            dve_hT(2)
            done = dve.done

            def first_max(oh, vals, m, n):
                done(V.reduce_max(m, vals, AX.X))
                done(V.tensor_tensor(oh, vals, bc(m, n), ALU.is_equal))
                c = r_cand[:, :, 0:n]
                done(V.scalar_tensor_tensor(c, oh, -1024.0, bt(iota[:, 0:n], n), MUL, ADD))
                done(V.tensor_reduce(r_mi, c, AX.X, MIN))
                done(V.tensor_tensor(oh, c, bc(r_mi, n), ALU.is_equal))

            bank = take(V, ("logits",))
            empty(V, "dve", V.tensor_tensor(r_lg, b3(bank[:, 0:144], 36), bt(wrb, 36), ADD), ("logits",))
            lg_g = r_lg[:, :, 0:4]
            first_max(r_ohg, lg_g, r_m, 4)
            done(V.tensor_tensor(r_eg, lg_g, bc(r_m, 4), SUB))
            eng.sem_inc(s_rt_in, 1)
            for g in range(4):
                in_g = r_lg[:, :, 4 + 8 * g:12 + 8 * g]
                hot = r_ohg[:, :, g:g + 1].to_broadcast([P, TT, 8])
                if not g:
                    done(V.tensor_tensor(r_el, in_g, hot, MUL))
                else:
                    done(V.tensor_tensor(r_el2, in_g, hot, MUL))
                    done(V.tensor_tensor(r_el, r_el, r_el2, ADD))
            first_max(r_oh1, r_el, r_m1, 8)
            done(V.scalar_tensor_tensor(r_el2, r_oh1, NEG, r_el, MUL, ADD))
            first_max(r_oh2, r_el2, r_m, 8)
            done(V.tensor_tensor(r_d, r_m, r_m1, SUB))
            eng.sem_inc(s_rt_in, 1)
            for k, oh in enumerate((r_oh1, r_oh2)):
                for g in range(4):
                    last = V.tensor_tensor(r_oh[k][:, :, 8 * g:8 * g + 8], oh, r_ohg[:, :, g:g + 1].to_broadcast([P, TT, 8]), MUL)
            done(last)
            done(V.tensor_tensor(chosen, r_oh[0], r_oh[1], ADD))
            eng.sem_inc(s_chosen, 1)
            eng.wait_ge(s_rt_exp, 2)
            done(V.reduce_sum(r_pg, r_eg, AX.X))
            done(V.tensor_scalar(r_w1, r_d, 1.0, None, ADD))
            done(V.tensor_tensor(r_w1, r_w1, r_pg, MUL))
            done(V.reciprocal(wts[:, 0, :], r_w1))
            done(V.tensor_tensor(wts[:, 1, :], wts[:, 0, :], r_d, MUL))
            bank = take(V, ("rank",))
            empty(V, "dve", V.tensor_copy(r_rank, bank[:, 0:5 * NE]), ("rank",))
            cnt = r_rank[:, 4 * NE:5 * NE]
            done(V.tensor_scalar(r_nov, cnt, float(MT), None, ALU.is_gt))
            for j in range(2, SEQ // MT):
                done(V.scalar_tensor_tensor(r_nov, cnt, float(MT * j), r_nov, ALU.is_gt, ADD))
            done(V.tensor_tensor_scan(r_incl, r_ones, r_nov, 0.0, MUL, ADD))
            done(V.tensor_tensor(r_xs, r_incl, r_nov, SUB))
            V.tensor_copy(ov_first[:, 0:NE], r_xs[0:1, :])
            V.tensor_copy(ov_first[:, NE:NE + 1], r_incl[0:1, NE - 1:NE])
            for k in range(2):
                for dst, src in ((r_rk, b3(r_rank[:, 0:4 * NE], NE)), (r_xk, bt(r_xs, NE)), (r_ek, bt(iota[:, 0:NE], NE))):
                    done(V.tensor_tensor(r_t, r_oh[k], src, MUL))
                    done(V.reduce_sum(dst, r_t, AX.X))
                done(V.tensor_scalar(r_q, r_rk, float(MT), None, ALU.is_ge))
                for j in range(2, SEQ // MT):
                    done(V.scalar_tensor_tensor(r_q, r_rk, float(MT * j), r_q, ALU.is_ge, ADD))
                done(V.scalar_tensor_tensor(r_pos, r_q, -float(MT), r_rk, MUL, ADD))
                done(V.tensor_tensor(r_xk, r_xk, r_q, ADD))
                done(V.scalar_tensor_tensor(r_xk, r_xk, float(NE - 1), r_ek, ADD, SUB))
                done(V.tensor_scalar(r_q, r_q, 0.0, None, ALU.is_gt))
                done(V.tensor_tensor(r_xk, r_xk, r_q, MUL))
                done(V.tensor_tensor(r_tile, r_xk, r_ek, ADD))
                done(V.scalar_tensor_tensor(r_rk, r_tile, float(MT), r_pos, MUL, ADD))
                V.tensor_copy(dest[:, k, :], r_rk)
                for t in range(TT):
                    V.tensor_scalar(hot_pos[:, 2 * t + k, :], iota, r_pos[:, t:t + 1], tok1[:, t:t + 1], ALU.is_equal, MUL)
                    last = V.tensor_scalar(hot_tile[:, 2 * t + k, :], iota[:, 0:NE + NOV], r_tile[:, t:t + 1], None, ALU.is_equal)
                done(last)
            eng.sem_inc(s_hot, 1)
            bank = take(V, ("slots",))
            v = r_v[0:MT]
            done(V.tensor_scalar(v, bank[0:MT, 0:NE + NOV], 0.0, 1024.0, ALU.is_equal, MUL))
            empty(V, "dve", V.scalar_tensor_tensor(v, bank[0:MT, 0:NE + NOV], -1.0, v, ADD, ADD), ("slots",))
            done(V.tensor_copy(slots[:, :], v))
            eng.sem_inc(s_routed, 1)

        U = 3
        ROUNDS, REST = NE // U, NE % U
        slot_w = [arena[:, 12288 * u:12288 * (u + 1)] for u in range(U)]
        wgu = [w[:, 0:8192].rearrange("p (a k n) -> p a k n", a=2, k=KD) for w in slot_w]
        wdn = [w[:, 8192:12288].rearrange("p (a n) -> p a n", a=4) for w in slot_w]
        yflat = yT[:, :, :].rearrange("p k t -> p (k t)")
        hflat = hT[:, :, :].rearrange("p k t -> p (k t)")

        class Tile:
            def __init__(self, u, xg, xT, hid, hidT, yo):
                self.xg, self.xT = xg, xT.rearrange("p (k m) -> p k m", m=MT)
                self.hid, self.hidT = hid, hidT.rearrange("p (j h m) -> p j h m", h=2, m=MT)
                self.yo = yo
                self.gathered, self.xf, self.stored = (sem(f"{n}_{u}") for n in (
                    "rows_gathered", "x_turned", "rows_stored"))

        class Steps:
            def __init__(self, which):
                (self.xT, self.gate_up, self.exp, self.hid, self.turned, self.hidT, self.down, self.rows,
                 self.own, self.xT_own) = (sem(f"{which}_{n}") for n in (
                     "xT_made", "gate_up_done", "gate_exp_made", "hidden_made", "hidden_turned",
                     "hiddenT_made", "down_done", "rows_made", "vector_steps", "xT_scaled"))

        first, more_ = Steps("first"), Steps("extra")

        tiles = [Tile(u, yflat[0:MT, 1024 * u:1024 * u + 1024], hflat[:, 512 * u:512 * u + 512],
                      hflat[:, 1536 + 256 * u:1792 + 256 * u], yflat[:, 3072 + 256 * u:3328 + 256 * u],
                      hflat[:, 2304 + 512 * u:2816 + 512 * u]) for u in range(U)]
        extra = Tile("extra", side[0:MT, 0:1024], side[:, 1024:1536], side[:, 1536:1792], side[:, 1792:2048],
                     cactB[:, :, :].rearrange("p k m -> p (k m)"))
        w_gu = [sem(f"gate_up_loaded_{u}") for u in range(U)]
        w_dn = [sem(f"down_loaded_{u}") for u in range(U)]
        w_free = [sem(f"weights_used_{u}") for u in range(U)]
        s_fin, s_ld = [sem(f"results_gathered_{t}") for t in range(TT)], sem("final_rows_loaded")
        s_x3, s_r3, s_rows = sem("x_final"), sem("x_final_norm"), sem("rows_out")
        s_passed = sem("waits_passed")
        s_picked = [sem("first_indices_picked"), sem("extra_indices_picked")]
        idx_col = sb("idx_col", [MT, U + 1], u32)

        def stand_alone(eng):
            eng.sem_inc(s_passed, 1)

        def experts(eng, body):
            for u in range(U):
                body(0, u, u)
            with eng.Fori(1, ROUNDS) as it:
                for u in range(U):
                    body(it, u, it * U + u)
            for u in range(REST):
                body(ROUNDS, u, ROUNDS * U + u)

        def before(it, u):
            return (it, u - 1) if u else (it - 1, U - 1)

        def after(it, u):
            return (it, u + 1) if u + 1 < U else (it + 1, 0)

        LAST = before(ROUNDS, REST) if REST else (ROUNDS - 1, U - 1)

        def extras(eng, e, body):
            lo = eng.value_load(ov_first[0:1, bass.ds(e, 1)], min_val=0, max_val=NOV)
            hi = eng.value_load(ov_first[0:1, bass.ds(e + 1, 1)], min_val=0, max_val=NOV)
            with eng.If(lo < hi):
                with eng.Fori(lo, hi) as o:
                    body(o)

        def sp_experts(eng):
            def body(it, u, e):
                eng.wait_ge(w_free[u], it + 1)
                for a, name in enumerate(("w_gate", "w_up")):
                    eng.dma_start(wgu[u][:, a, :, :], A[name].rearrange("e (p k) n -> e p k n", k=KD)[bass.ds(e, 1)]
                                  .rearrange("o p k n -> (o p) k n")).then_inc(w_gu[u], 16)
                eng.dma_start(wdn[u], A["w_down"].rearrange("e (a p) n -> e p a n", p=P)[bass.ds(e, 1)]
                              .rearrange("o p a n -> (o p) a n")).then_inc(w_dn[u], 16)
            experts(eng, body)
            for t in range(TT):
                eng.wait_ge(s_rows, t + 1)
                eng.dma_start(A["out"][CH(t), :], yg[:, 2 * t, :]).then_inc(s_out, 16)
            eng.wait_ge(s_out, 16 * TT)

        def pool_experts(eng):
            done = pool.done
            eng.wait_ge(s_xn, 3)
            eng.dma_start(xn_dram.rearrange("(t p) d -> p t d", p=P), xn).then_inc(s_xnst, 16)
            eng.wait_ge(s_xnst, 16)
            eng.wait_ge(filled, fill_at[("hT", 2, KD - 1)] + 1)
            done(G.memset(yflat[0:MT, 0:3072], 0.0))
            eng.wait_ge(s_routed, 1)
            done(G.memset(extra.xg, 0.0))

            def gather(tile, i, e, picked, n):
                G.tensor_copy(idx_col[:, i:i + 1], slots[:, bass.ds(e, 1)]).then_inc(picked, 1)
                eng.wait_ge(picked, n + 1)
                stand_alone(eng)
                eng.indirect_dma_start(tile.xg, None, xn_dram, bass.IndirectOffsetOnAxis(ap=idx_col[:, i:i + 1], axis=0),
                                       bounds_check=SEQ - 1, oob_is_err=False).then_inc(tile.gathered, 16)

            def more(o):
                eng.wait_ge(extra.xf, o + 1)
                gather(extra, U, o + NE, s_picked[1], o)

            def body(it, u, e):
                if not (isinstance(e, int) and e == NE - 1):
                    it1, u1 = after(it, u)
                    eng.wait_ge(tiles[u1].xf, it1 + 1)
                    gather(tiles[u1], u1, e + 1, s_picked[0], e + 1)
                extras(eng, e, more)
            eng.wait_ge(tiles[0].xf, 1)
            gather(tiles[0], 0, 0, s_picked[0], 0)
            experts(eng, body)
            eng.wait_ge(w_free[2], ROUNDS + 1)
            eng.dma_start(gateF, bass.AP(mod_dram.tensor, 8 * DM, [[0, P], [1, DM]])).then_inc(s_ld, 16)
            eng.dma_start(finalG, bass.AP(A["final_g"].tensor, 0, [[0, P], [1, DM]])).then_inc(s_ld, 16)
            for u in range(U):
                eng.wait_ge(tiles[u].stored, 1 + 32 * (ROUNDS + (u < REST)))
            n = eng.value_load(ov_first[0:1, NE:NE + 1], min_val=0, max_val=NOV)
            eng.wait_ge(extra.stored, n * 32 + 1)
            stand_alone(eng)
            for t in range(TT):
                for k in range(2):
                    eng.indirect_dma_start(yg[:, 2 * t + k, :], None, y_dram,
                                           bass.IndirectOffsetOnAxis(ap=dest[:, k, t:t + 1], axis=0),
                                           bounds_check=(NE + NOV) * MT - 1, oob_is_err=False).then_inc(s_fin[t], 16)

        yg = arena[:, 24576:24576 + 8192].rearrange("p (n d) -> p n d", d=DM)
        gateF, finalG, ftmp = (arena[:, 24576 + 8192 + 1024 * i:24576 + 9216 + 1024 * i] for i in range(3))

        def pe_experts(eng):
            for by in ("act", "dve"):
                eng.wait_ge(emptied[by], len(given[by]))
            for tile in (*tiles, extra):
                eng.sem_inc(tile.xf, 1)

            def turn_rows(tile, steps, n, turn):
                eng.wait_ge(steps.xT, n + 1)
                eng.wait_ge(tile.gathered, (turn + 1) * 16)
                stand_alone(eng)
                for k in range(KD):
                    last = T.transpose(banks[0][:, MT * k:MT * k + MT], tile.xg[:, k::KD], ident[0:MT, 0:MT])
                last.then_inc(tile.xf, 1)

            def gate_up(tile, steps, u, n):
                eng.wait_ge(steps.xT, n + 2)
                for k in range(KD):
                    for h in range(2):
                        last = T.matmul(banks[1 + u][MT * h:MT * h + MT, :], tile.xT[:, k, :],
                                        wgu[u][:, :, k, 256 * h:256 * h + 256], start=k == 0, stop=k == KD - 1)
                last.then_inc(steps.gate_up, 1)

            def turn_hidden(tile, steps, n):
                eng.wait_ge(steps.hid, n + 1)
                for j in range(2):
                    last = T.transpose(banks[4][:, CH(j)], tile.hid[:, CH(j)], ident[:, :])
                last.then_inc(steps.turned, 1)

            def down(tile, steps, u, n):
                eng.wait_ge(steps.hidT, n + 1)
                for a in range(4):
                    h, j = divmod(a, 2)
                    for q in range(2):
                        last = T.matmul(banks[5 + u][MT * q:MT * q + MT, :], tile.hidT[:, j, h, :],
                                        wdn[u][:, a, 512 * q:512 * q + 512], start=a == 0, stop=a == 3)
                last.then_inc(steps.down, 1)

            def finish(it, u, e):
                eng.wait_ge(w_dn[u], (it + 1) * 16)
                down(tiles[u], first, u, e)

                def more(o):
                    eng.wait_ge(first.rows, e + 1)
                    turn_rows(extra, more_, o, o)
                    gate_up(extra, more_, u, o)
                    turn_hidden(extra, more_, o)
                    down(extra, more_, u, o)
                    eng.wait_ge(more_.rows, o + 1)
                extras(eng, e, more)
                eng.wait_ge(first.down, e + 1)
                eng.sem_inc(w_free[u], 1)

            def body(it, u, e):
                it0, u0 = before(it, u)
                begun = isinstance(e, int) and e == 0
                if not begun:
                    turn_hidden(tiles[u0], first, e - 1)
                eng.wait_ge(w_gu[u], (it + 1) * 32)
                gate_up(tiles[u], first, u, e)
                if not begun:
                    finish(it0, u0, e - 1)
                if not (isinstance(e, int) and e == NE - 1):
                    it1, u1 = after(it, u)
                    turn_rows(tiles[u1], first, e + 1, it1)
            turn_rows(tiles[0], first, 0, 0)
            experts(eng, body)
            turn_hidden(tiles[LAST[1]], first, NE - 1)
            finish(LAST[0], LAST[1], NE - 1)

        def act_experts(eng):
            for tile in (*tiles, extra):
                eng.sem_inc(tile.stored, 1)

            def gate_exp(tile, steps, u, n):
                eng.wait_ge(steps.gate_up, n + 1)
                S.activation(tile.hid, banks[1 + u][:, 0:256], ACT.Exp, scale=-1.0).then_inc(steps.exp, 1)

            def hidden_out(tile, steps, n):
                eng.wait_ge(steps.turned, n + 1)
                S.activation(tile.hidT.rearrange("p j h m -> p (j h m)"), banks[4][:, 0:256], ACT.Copy).then_inc(steps.hidT, 1)

            def rows_out(tile, steps, u, n, turn, row):
                eng.wait_ge(steps.down, n + 1)
                eng.wait_ge(tile.stored, turn * 32 + 1)
                S.activation(tile.yo, banks[5 + u][:, :], ACT.Copy).then_inc(steps.rows, 1)
                eng.wait_ge(steps.rows, n + 1)
                for q in range(2):
                    eng.dma_start(y_dram[bass.ds(row * MT, MT), 512 * q:512 * q + 512],
                                  tile.yo[MT * q:MT * q + MT, :]).then_inc(tile.stored, 16)

            def finish(it, u, e):
                rows_out(tiles[u], first, u, e, it, e)

                def more(o):
                    gate_exp(extra, more_, u, o)
                    hidden_out(extra, more_, o)
                    rows_out(extra, more_, u, o, o, o + NE)
                extras(eng, e, more)

            def body(it, u, e):
                it0, u0 = before(it, u)
                begun = isinstance(e, int) and e == 0
                if not begun:
                    hidden_out(tiles[u0], first, e - 1)
                gate_exp(tiles[u], first, u, e)
                if not begun:
                    finish(it0, u0, e - 1)
            experts(eng, body)
            hidden_out(tiles[LAST[1]], first, NE - 1)
            finish(LAST[0], LAST[1], NE - 1)

        def dve_experts(eng):
            A2, B2 = (a.rearrange("p (k o) -> p k o", o=1).to_broadcast([P, KD, MT]) for a in (AB[2], modc[4]))

            for steps in (first, more_):
                eng.sem_inc(steps.xT, 1)

            def rows_in(tile, steps, n, turn):
                eng.wait_ge(tile.xf, turn + 2)
                V.tensor_tensor(tile.xT, b3(banks[0][:, :], MT), A2, MUL).then_inc(steps.xT_own, 1)
                eng.wait_ge(steps.xT_own, n + 1)
                V.tensor_tensor(tile.xT, tile.xT, B2, ADD).then_inc(steps.xT, 1)

            def hidden(tile, steps, u, n):
                bank = banks[1 + u]
                eng.wait_ge(steps.exp, n + 1)
                V.tensor_scalar(tile.hid, tile.hid, 1.0, None, ADD).then_inc(steps.own, 1)
                eng.wait_ge(steps.own, n * 3 + 1)
                V.reciprocal(tile.hid, tile.hid).then_inc(steps.own, 1)
                eng.wait_ge(steps.own, n * 3 + 2)
                V.tensor_tensor(tile.hid, tile.hid, bank[:, 0:256], MUL).then_inc(steps.own, 1)
                eng.wait_ge(steps.own, n * 3 + 3)
                V.tensor_tensor(tile.hid, tile.hid, bank[:, 256:512], MUL).then_inc(steps.hid, 1)

            def finish(u, e):
                def more(o):
                    rows_in(extra, more_, o, o)
                    hidden(extra, more_, u, o)
                extras(eng, e, more)

            def body(it, u, e):
                hidden(tiles[u], first, u, e)
                if not (isinstance(e, int) and e == 0):
                    finish(before(it, u)[1], e - 1)
                if not (isinstance(e, int) and e == NE - 1):
                    it1, u1 = after(it, u)
                    rows_in(tiles[u1], first, e + 1, it1)
            rows_in(tiles[0], first, 0, 0)
            experts(eng, body)
            finish(LAST[1], NE - 1)

        def act_final(eng):
            for t in range(TT):
                eng.wait_ge(s_x3, t + 1)
                act.done(S.activation(yg[:, 2 * t + 1, :], X[:, t, :], ACT.Square, accum_out=ss[:, t:t + 1]))
                act.done(S.activation(rstd[:, t:t + 1], ss[:, t:t + 1], ACT.Ln, scale=1.0 / DM, bias=eps_rms))
                act.done(S.activation(rstd[:, t:t + 1], rstd[:, t:t + 1], ACT.Exp, scale=-0.5))
                eng.sem_inc(s_r3, 1)

        def dve_final(eng):
            eng.wait_ge(s_ld, 32)

            def rows_out(t):
                eng.wait_ge(s_r3, t + 1)
                dve.done(V.scalar_tensor_tensor(yg[:, 2 * t, :], X[:, t, :], rstd[:, t:t + 1], finalG, MUL, MUL))
                eng.sem_inc(s_rows, 1)

            for t in range(TT):
                a, b = yg[:, 2 * t, :], yg[:, 2 * t + 1, :]
                eng.wait_ge(s_fin[t], 32)
                dve.done(V.tensor_scalar(a, a, wts[:, 0, t:t + 1], None, MUL))
                dve.done(V.scalar_tensor_tensor(a, b, wts[:, 1, t:t + 1], a, MUL, ADD))
                dve.done(V.tensor_tensor(a, a, gateF, MUL))
                dve.done(V.tensor_tensor(X[:, t, :], X[:, t, :], a, ADD))
                eng.sem_inc(s_x3, 1)
                if t:
                    rows_out(t - 1)
            rows_out(TT - 1)


        block = ctx.enter_context(nc.Block())

        @block.sync
        def _(eng):
            sp_block1(eng)
            sp_experts(eng)

        @block.gpsimd
        def _(eng):
            pool_block1(eng)
            pool_block2(eng)
            pool_experts(eng)

        @block.scalar
        def _(eng):
            act_block1(eng)
            act_block2(eng)
            eng.wait_ge(s_blk1, 2)
            act_norm(2)
            act_router(eng)
            act_experts(eng)
            act_final(eng)

        @block.tensor
        def _(eng):
            pe_block1(eng)
            pe_block2(eng)
            pe_experts(eng)

        @block.vector
        def _(eng):
            dve_block1(eng)
            dve_block2(eng)


_OUT = ((SEQ, DM), "float32")


def lay_out(inputs):
    import numpy as np
    a = {k: np.asarray(v) for k, v in inputs.items()}
    w_in_2 = a["w_in_2"][0]
    arrays = {
        "x": a["x"], "cols": pack_columns(a), "rel_rev": a["rel_bias"][0][:, ::-1],
        "w_ada": a["w_ada"][0], "b_ada": a["b_ada"][0], "ada_w_2": a["ada_w_2"][0], "ada_b_2": a["ada_b_2"][0],
        "w_in": a["w_in"][0], "w2": a["w2"][0], "a2": a["a2"][0], "w_out": a["w_out"][0],
        "w_in_2": w_in_2, "w_dtf": np.concatenate([w_in_2[:, 1536:1544], w_in_2[:, 2312:2316]], axis=1),
        "w_out_2": a["w_out_2"][0],
        "w_router": np.concatenate([a["w_router_group_2"][0], a["w_router_expert_2"][0]], axis=1),
        "b_router": np.concatenate([a["b_router_group_2"][0], a["b_router_expert_2"][0]]),
        "w_gate": a["w_gate_2"][0], "w_up": a["w_up_2"][0], "w_down": a["w_down_2"][0],
        "final_g": a["final_norm_g_2"],
    }
    return {k: np.ascontiguousarray(v) for k, v in arrays.items()}


def kernel(**inputs):
    import concourse.bacc as _bacc
    from concourse import mybir as _mybir
    from concourse.bass_utils import run_bass_kernel_spmd as _run

    nc = _bacc.Bacc("TRN2", target_bir_lowering=False, num_devices=1)
    arrays = lay_out(inputs)
    aps = {k: nc.dram_tensor(f"in_{k}", v.shape, _mybir.dt.from_np(v.dtype), kind="ExternalInput").ap()
           for k, v in arrays.items()}
    aps["out"] = nc.dram_tensor("out_rows", _OUT[0], _mybir.dt.float32, kind="ExternalOutput").ap()
    build_program(nc, aps)
    r = _run(nc, [{f"in_{k}": v for k, v in arrays.items()}], core_ids=[0])
    return r.results[0]["out_rows"].reshape(1, SEQ, DM)
```
